# Optimizing a Trainium2 kernel written in Bass

```python
import jax, jax.numpy as jnp
from jax import lax
import numpy as np

D_MODEL = 1024
BATCH = 1
SEQ = 512
DEPTH = 1

N_MEM = 256
SC_WIDTH = D_MODEL
SC_KERNEL = 3
CF_WIDTH = D_MODEL
CF_KERNEL = 31
XA_HEADS = 4
XA_HEAD_DIM = D_MODEL // XA_HEADS
PEER_HEADS = 8
PEER_NKEYS = 128
PEER_TOPK = 16
PEER_QDIM = 256
PEER_HALF = PEER_QDIM // 2
PEER_EXPERTS = PEER_NKEYS * PEER_NKEYS
PEER_CHUNK = 128
IN_COLS = 3 * SC_WIDTH + 2 * CF_WIDTH + 2 * D_MODEL
EPS = 1e-6


def rms_norm(x, g):
    xf = x.astype(jnp.float32)
    y = xf * lax.rsqrt(jnp.mean(xf * xf, axis=-1, keepdims=True) + EPS)
    return (y * g.astype(jnp.float32)).astype(x.dtype)

def layer_norm(x, g, b):
    xf = x.astype(jnp.float32)
    mu = jnp.mean(xf, axis=-1, keepdims=True)
    var = jnp.mean(jnp.square(xf - mu), axis=-1, keepdims=True)
    y = (xf - mu) * lax.rsqrt(var + EPS)
    return (y * g.astype(jnp.float32) + b.astype(jnp.float32)).astype(x.dtype)

def causal_depthwise_conv(x, w):
    k, c = w.shape
    return lax.conv_general_dilated(
        x, w.reshape(k, 1, c).astype(x.dtype), window_strides=(1,), padding=[(k - 1, 0)],
        dimension_numbers=('NWC', 'WIO', 'NWC'), feature_group_count=c)

def conv_mixers(h, w_in, cf_b_pw1, sc_conv_w, sc_w_out, cf_conv_w, cf_conv_b, cf_ln_g, cf_ln_b,
                cf_w_pw2, cf_b_pw2, w_mix_out):
    proj = jnp.einsum('bsd,dc->bsc', h, w_in)
    cuts = [SC_WIDTH, 2 * SC_WIDTH, 3 * SC_WIDTH, 3 * SC_WIDTH + CF_WIDTH,
            3 * SC_WIDTH + 2 * CF_WIDTH, 3 * SC_WIDTH + 2 * CF_WIDTH + D_MODEL]
    sc_b, sc_c, sc_x, cf_a, cf_g, gate_sc, gate_cf = jnp.split(proj, cuts, axis=-1)
    y_sc = sc_b * causal_depthwise_conv(sc_c * sc_x, sc_conv_w)
    y_sc = jnp.einsum('bsc,cd->bsd', y_sc, sc_w_out)
    cf = (cf_a + cf_b_pw1[:CF_WIDTH]) * jax.nn.sigmoid(cf_g + cf_b_pw1[CF_WIDTH:])
    cf = causal_depthwise_conv(cf, cf_conv_w) + cf_conv_b
    cf = jax.nn.silu(layer_norm(cf, cf_ln_g, cf_ln_b))
    y_cf = jnp.einsum('bsc,cd->bsd', cf, cf_w_pw2) + cf_b_pw2
    merged = jax.nn.sigmoid(gate_sc) * y_sc + jax.nn.sigmoid(gate_cf) * y_cf
    return jnp.einsum('bsd,de->bse', merged, w_mix_out)

def memory_cross_attention(h, mem_n, w_q, w_kv, w_xo):
    b, s, _ = h.shape
    m = mem_n.shape[1]
    q = jnp.einsum('bsd,de->bse', h, w_q).reshape(b, s, XA_HEADS, XA_HEAD_DIM)
    kv = jnp.einsum('bmd,de->bme', mem_n, w_kv).reshape(b, m, 2, XA_HEADS, XA_HEAD_DIM)
    k, v = kv[:, :, 0], kv[:, :, 1]
    scores = jnp.einsum('bshd,bmhd->bhsm', q, k).astype(jnp.float32) * (XA_HEAD_DIM ** -0.5)
    probs = jax.nn.softmax(scores, axis=-1).astype(v.dtype)
    o = jnp.einsum('bhsm,bmhd->bshd', probs, v).reshape(b, s, XA_HEADS * XA_HEAD_DIM)
    return jnp.einsum('bse,ed->bsd', o, w_xo)

def peer_ffn(h, w_pq, subkeys, u, v):
    b, s, d = h.shape
    q = jnp.einsum('bsd,dq->bsq', h, w_pq).reshape(b, s, PEER_HEADS, 2, PEER_HALF)
    sub_scores = jnp.einsum('bshpc,pnc->bshpn', q, subkeys).astype(jnp.float32)
    top_s, top_i = lax.top_k(sub_scores, PEER_TOPK)
    n_cand = PEER_TOPK * PEER_TOPK
    cand_s = (top_s[..., 0, :, None] + top_s[..., 1, None, :]).reshape(b, s, PEER_HEADS, n_cand)
    cand_i = (top_i[..., 0, :, None] * PEER_NKEYS + top_i[..., 1, None, :]).reshape(b, s, PEER_HEADS, n_cand)
    fin_s, fin_pos = lax.top_k(cand_s, PEER_TOPK)
    expert_idx = jnp.take_along_axis(cand_i, fin_pos, axis=-1)
    gates = jax.nn.softmax(fin_s, axis=-1).astype(h.dtype)
    n_chunks = (b * s) // PEER_CHUNK
    h_c = h.reshape(n_chunks, PEER_CHUNK, d)
    e_c = expert_idx.reshape(n_chunks, PEER_CHUNK, PEER_HEADS, PEER_TOPK)
    g_c = gates.reshape(n_chunks, PEER_CHUNK, PEER_HEADS, PEER_TOPK)

    def chunk(args):
        hc, ec, gc = args
        u_sel = jnp.take(u, ec, axis=0)
        act = jax.nn.gelu(jnp.einsum('chkd,cd->chk', u_sel, hc), approximate=False) * gc
        v_sel = jnp.take(v, ec, axis=0)
        return jnp.einsum('chk,chkd->cd', act, v_sel)

    out = lax.map(chunk, (h_c, e_c, g_c))
    return out.reshape(b, s, d)

def first_inputs(seed: int = 0) -> dict:
    key = jax.random.key(seed)
    ks = jax.random.split(key, 26)
    L = DEPTH

    def nrm(k, shape, scale):
        return jax.random.normal(k, shape, jnp.float32) * scale

    def gain(k, shape):
        return 1.0 + 0.02 * jax.random.normal(k, shape, jnp.float32)

    return {
        'x': nrm(ks[0], (BATCH, SEQ, D_MODEL), 1.0),
        'mem': nrm(ks[1], (BATCH, N_MEM, D_MODEL), 1.0),
        'norm_mix_g': gain(ks[2], (L, D_MODEL)),
        'w_in': nrm(ks[3], (L, D_MODEL, IN_COLS), D_MODEL ** -0.5),
        'cf_b_pw1': nrm(ks[4], (L, 2 * CF_WIDTH), 0.02),
        'sc_conv_w': nrm(ks[5], (L, SC_KERNEL, SC_WIDTH), SC_KERNEL ** -0.5),
        'sc_w_out': nrm(ks[6], (L, SC_WIDTH, D_MODEL), SC_WIDTH ** -0.5),
        'cf_conv_w': nrm(ks[7], (L, CF_KERNEL, CF_WIDTH), CF_KERNEL ** -0.5),
        'cf_conv_b': nrm(ks[8], (L, CF_WIDTH), 0.02),
        'cf_ln_g': gain(ks[9], (L, CF_WIDTH)),
        'cf_ln_b': nrm(ks[10], (L, CF_WIDTH), 0.02),
        'cf_w_pw2': nrm(ks[11], (L, CF_WIDTH, D_MODEL), CF_WIDTH ** -0.5),
        'cf_b_pw2': nrm(ks[12], (L, D_MODEL), 0.02),
        'w_mix_out': nrm(ks[13], (L, D_MODEL, D_MODEL), D_MODEL ** -0.5),
        'norm_xa_g': gain(ks[14], (L, D_MODEL)),
        'norm_mem_g': gain(ks[15], (L, D_MODEL)),
        'w_q': nrm(ks[16], (L, D_MODEL, XA_HEADS * XA_HEAD_DIM), D_MODEL ** -0.5),
        'w_kv': nrm(ks[17], (L, D_MODEL, 2 * XA_HEADS * XA_HEAD_DIM), D_MODEL ** -0.5),
        'w_xo': nrm(ks[18], (L, XA_HEADS * XA_HEAD_DIM, D_MODEL), D_MODEL ** -0.5),
        'norm_peer_g': gain(ks[19], (L, D_MODEL)),
        'w_peer_q': nrm(ks[20], (L, D_MODEL, PEER_HEADS * PEER_QDIM), D_MODEL ** -0.5),
        'peer_subkeys': nrm(ks[21], (L, 2, PEER_NKEYS, PEER_HALF), PEER_HALF ** -0.5),
        'peer_u': nrm(ks[22], (L, PEER_EXPERTS, D_MODEL), D_MODEL ** -0.5),
        'peer_v': nrm(ks[23], (L, PEER_EXPERTS, D_MODEL), PEER_HEADS ** -0.5),
        'final_norm_g': gain(ks[24], (D_MODEL,)),
    }

def first_block(x, mem, norm_mix_g, w_in, cf_b_pw1, sc_conv_w, sc_w_out, cf_conv_w, cf_conv_b, cf_ln_g,
              cf_ln_b, cf_w_pw2, cf_b_pw2, w_mix_out, norm_xa_g, norm_mem_g, w_q, w_kv, w_xo, norm_peer_g,
              w_peer_q, peer_subkeys, peer_u, peer_v, final_norm_g):
    for l in range(DEPTH):
        x = x + conv_mixers(rms_norm(x, norm_mix_g[l]), w_in[l], cf_b_pw1[l], sc_conv_w[l], sc_w_out[l],
                            cf_conv_w[l], cf_conv_b[l], cf_ln_g[l], cf_ln_b[l], cf_w_pw2[l], cf_b_pw2[l],
                            w_mix_out[l])
        mem_n = rms_norm(mem, norm_mem_g[l])
        x = x + memory_cross_attention(rms_norm(x, norm_xa_g[l]), mem_n, w_q[l], w_kv[l], w_xo[l])
        x = x + peer_ffn(rms_norm(x, norm_peer_g[l]), w_peer_q[l], peer_subkeys[l], peer_u[l], peer_v[l])
    return rms_norm(x, final_norm_g)


N_META = 16
D_FF = 2816
RET_HEADS = 4
RET_DK = 256
RET_DV = 512
RET_CHUNK = 128
ATT_HEADS = 8
ATT_DH = 128
IDX_HEADS = 8
IDX_DH = 64
TOPK_MAX = 256
DSA_QBLOCK = 32
ROPE_THETA = 10000.0
RET_QK = RET_HEADS * RET_DK
RET_V = RET_HEADS * RET_DV
ATT_W = ATT_HEADS * ATT_DH
IDX_Q = IDX_HEADS * IDX_DH
IN_SPLITS = (RET_QK, RET_QK, RET_V, RET_V, ATT_W, ATT_W, ATT_W, IDX_Q, IDX_DH, IDX_HEADS, D_MODEL, D_MODEL)
D_IN = sum(IN_SPLITS)


def rmsnorm(x, g):
    xf = x.astype(jnp.float32)
    y = xf * lax.rsqrt(jnp.mean(xf * xf, axis=-1, keepdims=True) + EPS)
    return (y * g.astype(jnp.float32)).astype(x.dtype)

def rope(x, pos):
    d = x.shape[-1]
    inv_freq = ROPE_THETA ** (-jnp.arange(0, d, 2, dtype=jnp.float32) / d)
    ang = pos.astype(jnp.float32)[:, None] * inv_freq[None, :]
    cos = jnp.cos(ang)[:, None, :]
    sin = jnp.sin(ang)[:, None, :]
    xf = x.astype(jnp.float32)
    x1, x2 = xf[..., : d // 2], xf[..., d // 2:]
    return jnp.concatenate([x1 * cos - x2 * sin, x2 * cos + x1 * sin], axis=-1).astype(x.dtype)

def swiglu(u, w_gate, w_up, w_down):
    return (jax.nn.silu(u @ w_gate) * (u @ w_up)) @ w_down

def retention(q, k, v):
    out_dtype = v.dtype
    q, k, v = (a.astype(jnp.float32) for a in (q, k, v))
    B, H, T, _ = q.shape
    C = RET_CHUNK
    n = (T - N_META) // C
    log_g = jnp.log1p(-(2.0 ** (-5.0 - jnp.arange(H, dtype=jnp.float32))))

    def decay_matrix(c):
        i = jnp.arange(c, dtype=jnp.float32)
        diff = i[:, None] - i[None, :]
        return jnp.where(diff >= 0, jnp.exp(log_g[:, None, None] * jnp.maximum(diff, 0.0)), 0.0)

    qm, km, vm = q[:, :, :N_META], k[:, :, :N_META], v[:, :, :N_META]
    y_meta = jnp.einsum('bhqk,bhke->bhqe', jnp.einsum('bhqd,bhkd->bhqk', qm, km) * decay_matrix(N_META), vm)
    zeta_m = jnp.exp(log_g[:, None] * (N_META - 1.0 - jnp.arange(N_META, dtype=jnp.float32)))
    state0 = jnp.einsum('bhkd,bhke->bhde', km * zeta_m[..., None], vm)

    d_in = decay_matrix(C)
    pos_c = jnp.arange(C, dtype=jnp.float32)
    xi = jnp.exp(log_g[:, None] * (pos_c + 1.0))[..., None]
    zeta = jnp.exp(log_g[:, None] * (C - 1.0 - pos_c))[..., None]
    g_chunk = jnp.exp(log_g * C)[:, None, None]

    def to_chunks(a):
        return a[:, :, N_META:].reshape(B, H, n, C, a.shape[-1]).transpose(2, 0, 1, 3, 4)

    def step(state, qkv):
        qc, kc, vc = qkv
        inner = jnp.einsum('bhqk,bhke->bhqe', jnp.einsum('bhqd,bhkd->bhqk', qc, kc) * d_in, vc)
        cross = jnp.einsum('bhqd,bhde->bhqe', qc, state) * xi
        state = g_chunk * state + jnp.einsum('bhkd,bhke->bhde', kc * zeta, vc)
        return state, inner + cross

    _, y_chunks = lax.scan(step, state0, (to_chunks(q), to_chunks(k), to_chunks(v)))
    y_real = y_chunks.transpose(1, 2, 0, 3, 4).reshape(B, H, n * C, v.shape[-1])
    y = jnp.concatenate([y_meta, y_real], axis=2)
    y = y * lax.rsqrt(jnp.mean(y * y, axis=-1, keepdims=True) + EPS)
    return y.astype(out_dtype)

def dsa_attention(q, k, v, qi, ki, wi, k_top):
    B, T, H, dh = q.shape
    nb = -(-T // DSA_QBLOCK)
    t_pad = nb * DSA_QBLOCK
    pad = t_pad - T

    def blocks(a):
        a = jnp.pad(a, [(0, 0), (0, pad)] + [(0, 0)] * (a.ndim - 2))
        return a.reshape((B, nb, DSA_QBLOCK) + a.shape[2:]).swapaxes(0, 1)

    pos_blocks = jnp.arange(t_pad, dtype=jnp.int32).reshape(nb, DSA_QBLOCK)
    key_pos = jnp.arange(T, dtype=jnp.int32)
    meta_pos = jnp.arange(N_META, dtype=jnp.int32)
    k_meta, v_meta = k[:, :N_META], v[:, :N_META]
    scale = ATT_DH ** -0.5
    idx_scale = (IDX_DH ** -0.5) * (IDX_HEADS ** -0.5)
    gather = jax.vmap(lambda a, i: a[i])

    def one_block(args):
        qb, qib, wib, tq = args
        rel = jax.nn.relu(jnp.einsum('bqhd,bsd->bqhs', qib, ki))
        score = jnp.einsum('bqh,bqhs->bqs', wib, rel).astype(jnp.float32) * idx_scale
        admissible = (key_pos[None, :] >= N_META) & (key_pos[None, :] <= tq[:, None])
        score = jnp.where(admissible[None], score, -jnp.inf)
        _, sel = lax.top_k(score, k_top)
        sel_ok = (sel >= N_META) & (sel <= tq[None, :, None])
        k_sel = gather(k, sel)
        v_sel = gather(v, sel)
        s_meta = jnp.einsum('bqhd,bmhd->bhqm', qb, k_meta).astype(jnp.float32) * scale
        s_meta = jnp.where((meta_pos[None, :] <= tq[:, None])[None, None], s_meta, -jnp.inf)
        s_sel = jnp.einsum('bqhd,bqkhd->bhqk', qb, k_sel).astype(jnp.float32) * scale
        s_sel = jnp.where(sel_ok[:, None], s_sel, -jnp.inf)
        p = jax.nn.softmax(jnp.concatenate([s_meta, s_sel], axis=-1), axis=-1).astype(v.dtype)
        return (jnp.einsum('bhqm,bmhd->bqhd', p[..., :N_META], v_meta)
                + jnp.einsum('bhqk,bqkhd->bqhd', p[..., N_META:], v_sel))

    out = lax.map(one_block, (blocks(q), blocks(qi), blocks(wi), pos_blocks))
    return out.swapaxes(0, 1).reshape(B, t_pad, H, dh)[:, :T]

def hybrid_mixer(u, pos, k_top, w_in, w_ret_out, w_att_out, w_mix_out):
    B, T, _ = u.shape
    proj = u @ w_in
    offs = [int(o) for o in np.cumsum(IN_SPLITS)[:-1]]
    rq, rk, rv, rg, aq, ak, av, iq, ik, iw, g_ret, g_att = jnp.split(proj, offs, axis=-1)
    rq = rope(rq.reshape(B, T, RET_HEADS, RET_DK), pos)
    rk = rope(rk.reshape(B, T, RET_HEADS, RET_DK), pos) * (RET_DK ** -0.5)
    rv = rv.reshape(B, T, RET_HEADS, RET_DV)
    yr = retention(rq.transpose(0, 2, 1, 3), rk.transpose(0, 2, 1, 3), rv.transpose(0, 2, 1, 3))
    yr = yr.transpose(0, 2, 1, 3).reshape(B, T, RET_V)
    yr = (jax.nn.silu(rg) * yr) @ w_ret_out
    aq = rope(aq.reshape(B, T, ATT_HEADS, ATT_DH), pos)
    ak = rope(ak.reshape(B, T, ATT_HEADS, ATT_DH), pos)
    av = av.reshape(B, T, ATT_HEADS, ATT_DH)
    iq = rope(iq.reshape(B, T, IDX_HEADS, IDX_DH), pos)
    ik = rope(ik.reshape(B, T, 1, IDX_DH), pos)[:, :, 0]
    ya = dsa_attention(aq, ak, av, iq, ik, iw, k_top).reshape(B, T, ATT_W) @ w_att_out
    merged = jax.nn.sigmoid(g_ret) * yr + jax.nn.sigmoid(g_att) * ya
    return merged @ w_mix_out

def second_inputs(seed: int = 0) -> dict:
    key = jax.random.key(seed)
    ks = jax.random.split(key, 16)
    f32 = jnp.float32

    def dense(k, fan_in, fan_out):
        return jax.random.normal(k, (DEPTH, fan_in, fan_out), f32) * fan_in ** -0.5

    def gain(k, shape):
        return 1.0 + 0.02 * jax.random.normal(k, shape, f32)

    return {
        'x': jax.random.normal(ks[0], (BATCH, SEQ, D_MODEL), f32),
        'meta_tokens': jax.random.normal(ks[1], (N_META, D_MODEL), f32),
        'ffn1_norm': gain(ks[2], (DEPTH, D_MODEL)),
        'ffn1_w_gate': dense(ks[3], D_MODEL, D_FF),
        'ffn1_w_up': dense(ks[4], D_MODEL, D_FF),
        'ffn1_w_down': dense(ks[5], D_FF, D_MODEL),
        'mix_norm': gain(ks[6], (DEPTH, D_MODEL)),
        'w_in': dense(ks[7], D_MODEL, D_IN),
        'w_ret_out': dense(ks[8], RET_V, D_MODEL),
        'w_att_out': dense(ks[9], ATT_W, D_MODEL),
        'w_mix_out': dense(ks[10], D_MODEL, D_MODEL),
        'ffn2_norm': gain(ks[11], (DEPTH, D_MODEL)),
        'ffn2_w_gate': dense(ks[12], D_MODEL, D_FF),
        'ffn2_w_up': dense(ks[13], D_MODEL, D_FF),
        'ffn2_w_down': dense(ks[14], D_FF, D_MODEL),
        'final_norm': gain(ks[15], (D_MODEL,)),
    }

def second_block(x, meta_tokens, ffn1_norm, ffn1_w_gate, ffn1_w_up, ffn1_w_down, mix_norm, w_in, w_ret_out, w_att_out, w_mix_out, ffn2_norm, ffn2_w_gate, ffn2_w_up, ffn2_w_down, final_norm):
    B, L, D = x.shape
    k_top = min(TOPK_MAX, L // 4)
    meta = jnp.broadcast_to(meta_tokens.astype(x.dtype)[None], (B, N_META, D))
    h = jnp.concatenate([meta, x], axis=1)
    pos = jnp.arange(h.shape[1], dtype=jnp.int32)
    for l in range(DEPTH):
        h = h + 0.5 * swiglu(rmsnorm(h, ffn1_norm[l]), ffn1_w_gate[l], ffn1_w_up[l], ffn1_w_down[l])
        h = h + hybrid_mixer(rmsnorm(h, mix_norm[l]), pos, k_top, w_in[l], w_ret_out[l], w_att_out[l], w_mix_out[l])
        h = h + 0.5 * swiglu(rmsnorm(h, ffn2_norm[l]), ffn2_w_gate[l], ffn2_w_up[l], ffn2_w_down[l])
    y = rmsnorm(h, final_norm)
    return y[:, N_META:]


def setup_inputs(seed=0):
    out = dict(first_inputs(seed))
    for name, value in second_inputs(seed + 1).items():
        if name != "x":
            out[name + "_2"] = value
    return out


def reference(
    x, mem, norm_mix_g, w_in, cf_b_pw1, sc_conv_w, sc_w_out, cf_conv_w, cf_conv_b, cf_ln_g,
    cf_ln_b, cf_w_pw2, cf_b_pw2, w_mix_out, norm_xa_g, norm_mem_g, w_q, w_kv, w_xo, norm_peer_g,
    w_peer_q, peer_subkeys, peer_u, peer_v, final_norm_g, meta_tokens_2, ffn1_norm_2,
    ffn1_w_gate_2, ffn1_w_up_2, ffn1_w_down_2, mix_norm_2, w_in_2, w_ret_out_2, w_att_out_2,
    w_mix_out_2, ffn2_norm_2, ffn2_w_gate_2, ffn2_w_up_2, ffn2_w_down_2, final_norm_2,
):
    x = first_block(
        x, mem, norm_mix_g, w_in, cf_b_pw1, sc_conv_w, sc_w_out, cf_conv_w, cf_conv_b, cf_ln_g,
        cf_ln_b, cf_w_pw2, cf_b_pw2, w_mix_out, norm_xa_g, norm_mem_g, w_q, w_kv, w_xo,
        norm_peer_g, w_peer_q, peer_subkeys, peer_u, peer_v, final_norm_g,
    )
    return second_block(
        x, meta_tokens_2, ffn1_norm_2, ffn1_w_gate_2, ffn1_w_up_2, ffn1_w_down_2, mix_norm_2,
        w_in_2, w_ret_out_2, w_att_out_2, w_mix_out_2, ffn2_norm_2, ffn2_w_gate_2, ffn2_w_up_2,
        ffn2_w_down_2, final_norm_2,
    )


_drawn_inputs = setup_inputs


def setup_inputs(seed=0):
    import zlib

    import numpy as np

    out = dict(_drawn_inputs(seed))
    spreads = {}
    factors = {'cf_b_pw1': 3.134,
     'cf_ln_g': 2.995,
     'cf_ln_b': 3.303,
     'norm_xa_g': 5.986,
     'norm_mem_g': 5.062,
     'ffn1_norm_2': 5.226,
     'mix_norm_2': 3.769,
     'ffn2_norm_2': 7.048,
     'final_norm_2': 2.876}
    for name, (base, spread) in spreads.items():
        noise = np.random.default_rng([zlib.crc32(name.encode()), seed]).standard_normal(out[name].shape)
        drawn = base * np.exp(spread * noise) if base else spread * noise
        out[name] = __import__('jax').numpy.asarray(drawn.astype(out[name].dtype))
    for name, factor in factors.items():
        out[name] = (out[name] * factor).astype(out[name].dtype)
    return out
```

```python
from contextlib import ExitStack, contextmanager

import numpy as np

import concourse.bass as bass
from concourse import mybir

F32 = mybir.dt.float32
BF16 = mybir.dt.bfloat16
U32 = mybir.dt.uint32
ACT = mybir.ActivationFunctionType
ALU = mybir.AluOpType
AX = mybir.AxisListType.X

P = 128
D = 1024
KT = D // P
S = 512
QT = S // P
META = 16
T2 = S + META
HALF = T2 // 2
EPS = 1e-6
MEM = 256
MT = MEM // P
SC_K, CF_K = 3, 31
XA_HEADS, XA_DT = 4, 2
XA_SCALE = 256 ** -0.5
PEER_HEADS, TOPK = 8, 16
PICKS = PEER_HEADS * TOPK
EXPERTS = 128 * 128
FF = 2816
FT = FF // P
RET_HEADS, RET_DK, RET_DV = 4, 256, 512
ATT_HEADS = 8
ATT_SCALE = 128 ** -0.5
IDX_HEADS, IDX_DH = 8, 64
IDX_SCALE = (IDX_DH ** -0.5) * (IDX_HEADS ** -0.5)
KEEP = 128
THETA = 10000.0
RING = 4
SLOTS = 8
GROUP = 4
TURN = 4 * GROUP
FAR = -3.0e38
TAKEN = -3.2e38
FLOOR = -3.4e38
HIDE = -1.0e30

VECS = {}
_at = 0
for _name, _n in (("norm_mix", 8), ("b1a", 8), ("b1g", 8), ("sc_w", 8 * SC_K), ("cf_w", 8 * CF_K), ("cf_b", 8),
                  ("ln_g", 8), ("ln_b", 8), ("pw2_b", 8), ("norm_xa", 8), ("norm_mem", 8), ("norm_peer", 8),
                  ("final1", 8), ("ffn1", 8), ("mix2", 8), ("ffn2", 8), ("final2", 8)):
    VECS[_name] = _at
    _at += _n
NVEC = _at

FIXED = 3 * P + TOPK
TABLES = FIXED
DECAY = TABLES + 6 * T2
NCONST = DECAY + RET_HEADS * S
NORMS = 10


class Counter:

    def __init__(self):
        self.base, self.k, self.i, self.per = 0, 0, None, 0

    def enter(self, i, per):
        assert self.i is None
        self.base, self.k = self.base + self.k, 0
        self.i, self.per = i, per

    def leave(self, n):
        assert self.k == self.per, f"a turn of the loop counts {self.k}, not {self.per}"
        self.base, self.k, self.i = self.base + n * self.per, 0, None

    def value(self, shift=0):
        now = self.base + self.k + shift
        return now if self.i is None else self.i * self.per + now


class Ring(Counter):

    def __init__(self, n, first=0):
        super().__init__()
        self.n, self.first = n, first

    def take(self):
        now = self.base + self.k
        self.k += 1
        slot, before = now % self.n, now // self.n
        if self.i is not None:
            assert self.per % self.n == 0
            before = self.i * (self.per // self.n) + before
        return self.first + slot, before

    def taken(self):
        now = self.base + self.k
        return [(self.first + s, (now + self.n - 1 - s) // self.n) for s in range(self.n)]


class Chain(Counter):

    def __init__(self, eng, sem):
        super().__init__()
        self.eng, self.sem = eng, sem

    def step(self, ins):
        ins.then_inc(self.sem, 1)
        self.k += 1

    def wait(self, back=0):
        self.eng.wait_ge(self.sem, self.value(-back))


@contextmanager
def repeat(eng, n, counters):
    with eng.Fori(0, n) as i:
        for c, per in counters:
            c.enter(i, per)
        yield i
    for c, _ in counters:
        c.leave(n)


def row(t, index, a, b):
    return t[:, bass.ds(index, 1), a:b].rearrange("p a n -> p (a n)")


def build(nc, slabs_d, xT_d, memT_d, metaT_d, vecs_d, consts_d, consts16_d, subk_d, wi_d, peer_u_d, peer_v_d, out_d,
          n_slabs):
    ctx = ExitStack()
    with ctx:
        def sb(name, shape, dt=F32):
            return ctx.enter_context(nc.sbuf_tensor(name, shape, dt))

        def sem(name):
            return ctx.enter_context(nc.semaphore(name))

        slab = sb("slab", [P, RING, D])
        xT = sb("xT", [P, KT, T2])
        vecs = sb("vecs", [P, NVEC])
        fixed = sb("fixed", [P, FIXED])
        ident, ones = fixed[:, 0:P], fixed[:, P:2 * P]
        tri = fixed[:, 2 * P:3 * P]
        iota16 = fixed[:, 3 * P:FIXED]
        zeros = sb("zeros", [P, S], BF16)
        norm_ms = sb("norm_mean_square", [P, T2])
        norm_rs = sb("norm_recip_root", [P, T2])

        ARENA = 41600
        arena = sb("arena", [P, ARENA])

        class Part:
            def __init__(self, at=0):
                self.at = at

            def __call__(self, *shape, dt=F32, rows=P):
                n = int(np.prod(shape))
                v = arena[0:rows, self.at:self.at + n]
                self.at += n
                assert self.at <= ARENA, self.at
                if dt is not F32:
                    v = v.bitcast(dt)
                if len(shape) == 2:
                    v = v.rearrange("p (a b) -> p a b", a=shape[0])
                elif len(shape) == 3:
                    v = v.rearrange("p (a b c) -> p a b c", a=shape[0], b=shape[1])
                return v

        nT = arena[:, ARENA - KT * T2:ARENA].rearrange("p (k n) -> p k n", k=KT)
        part = Part()
        sq = part(KT, T2)
        merged = part(KT, S)
        shared = part.at
        scy = part(KT, S)
        cfc = part(KT, S)
        cfp = part(2, CF_K - 1 + S)
        scp = part(2, SC_K - 1 + S)
        sg = part(2, S)
        xs = part(2, S)
        sct = part(2, S)
        acc_e = part(S)
        acc_o = part(S)
        cfs = part(KT, S)
        mu = part(S)
        part = Part(shared)
        memT = part(KT, MEM)
        memN = part(KT, MEM)
        oT = part(KT, S)
        xk = part(2, XA_DT * MEM)
        xv = part(2, MT * 256)
        xq = part(2, XA_DT * S)
        xp = part(2, QT * MEM)
        xpt = part(2, MT * S)
        xmax = part(2, QT)
        xneg = part(2, QT)
        xsum = part(2, QT)
        xinv = part(2, QT)
        part = Part()
        sub_s = part(2 * PEER_HEADS * QT, P)
        subk = part(2, P)
        hrow = part(QT, D)
        eidx = part(QT, PICKS, dt=U32)
        gates = part(QT, PICKS)
        tk_in = part(2 * PEER_HEADS, P)
        tk_wk = part(2 * PEER_HEADS, P)
        cand = tk_in.rearrange("p (h a) n -> p h (a n)", h=PEER_HEADS)
        cand_wk = tk_wk.rearrange("p (h a) n -> p h (a n)", h=PEER_HEADS)
        onehot = tk_in.rearrange("p a (b n) -> p (a b) n", n=TOPK)
        tk_v = part(2 * PEER_HEADS, TOPK)
        tk_i = part(2 * PEER_HEADS, TOPK, dt=U32)
        tk_f = part(2 * PEER_HEADS, TOPK)
        fin_v = part(PEER_HEADS, TOPK)
        fin_e = part(PEER_HEADS, TOPK)
        fin_p = part(PEER_HEADS, TOPK, dt=U32)
        fin_a = part(PEER_HEADS, TOPK, dt=U32)
        fin_b = part(PEER_HEADS, TOPK, dt=U32)
        fin_af = part(PEER_HEADS, TOPK)
        fin_bf = part(PEER_HEADS, TOPK)
        fin_i0 = part(PEER_HEADS, TOPK)
        fin_i1 = part(PEER_HEADS, TOPK)
        fin_s = part(PEER_HEADS)
        fin_r = part(PEER_HEADS)
        gather = part.at
        pq = part(4, S)
        part = Part(gather)
        diag = part(SLOTS, P)
        dots = part(4, GROUP)
        acts = part(4, GROUP)
        coefs = part(4, GROUP)
        pick = part(4, GROUP, dt=U32)
        dump = part(D // 2, dt=BF16)
        out_rows = part(D)
        u_rows = part(SLOTS, D)
        v_rows = part(SLOTS, D)
        part = Part(shared)
        hid = part(FT, T2)
        silu = part(2, T2)
        part = Part(shared)
        cos_r, sin_r, cos_a, sin_a, cos_i, sin_i = (part(T2) for _ in range(6))
        key_bias = part(QT, S)
        yr = part(4 * RET_HEADS, S)
        work = key_bias[:, 1:QT, :]
        top8 = part(3, 8)
        mixer = part.at
        iq = part(4, S)
        ik = part(S)
        iw = part(QT, IDX_HEADS)
        wi = part(KT, IDX_HEADS)
        rope_t = part(2, T2)
        relu = part(2, S)
        score = part(3, S)
        part = Part(mixer)
        decay = part(RET_HEADS, S)
        decay_m = part(RET_HEADS, S, rows=META)
        rtm = part(4, META)
        rq = part(2, S)
        rk = part(2, S)
        rkm = part(2, META)
        rv = part(QT, S)
        rvm = part(S, rows=META)
        rg = part(4, S)
        rp = part(QT, S)
        rpm = part(S, rows=META)
        ry = part(4, S)
        rt = rp
        rsq = sq
        part = Part(mixer)
        gs = part(4, S)
        sga = part(KT, S)
        aq = part(S)
        ak = part(T2)
        at_t = part(2, S)
        at_tm = part(META)
        av = part(QT, P)
        avm = part(P, rows=META)
        ap_ = part(QT, T2)
        apt = part(QT, S)
        aptm = part(S, rows=META)
        amax = part(QT)
        aneg = part(QT)
        asum = part(QT)
        ainv = part(QT)
        at_y = part(2, S)
        oT2 = yr

        psum = ctx.enter_context(nc.psum_tensor("psum", [P, 8, 512], F32))

        slab_landed = [sem(f"slab_landed_{s}") for s in range(RING)]
        slab_used = sem("slab_used")
        bank_full = [sem(f"bank_full_{b}") for b in range(8)]
        bank_free = [sem(f"bank_free_{b}") for b in range(8)]
        loaded = sem("constants_loaded")
        mem_loaded = sem("memory_loaded")
        subk_loaded = sem("subkeys_loaded")
        mixer_loaded = sem("mixer_constants_loaded")
        decay_loaded = sem("decay_loaded")
        cleared = sem("pads_cleared")
        dve_step = sem("dve_step")
        dve_passed = sem("dve_passed_a_wait")
        pool_passed = sem("pool_passed_a_wait")
        norm_sq = sem("norm_squares")
        norm_mean = sem("norm_mean_ready")
        norm_root = sem("norm_root")
        norm_out = sem("norm_done")
        cf_done = sem("conformer_conv_done")
        cf_centred = sem("conformer_centred")
        cf_silu = sem("conformer_silu")
        merged_done = sem("merged_done")
        xa_bias = sem("xa_negative_max")
        xa_exp = sem("xa_exp")
        xa_probs = sem("xa_probs")
        gate_in = sem("peer_gate_shifted")
        gate_exp = sem("peer_gate_exp")
        picked = sem("peer_picked")
        pick_copied = sem("pick_copied")
        u_landed = [sem(f"u_landed_{j}") for j in range(SLOTS)]
        v_landed = [sem(f"v_landed_{j}") for j in range(SLOTS)]
        u_used = [sem(f"u_used_{j}") for j in range(SLOTS)]
        v_used = [sem(f"v_used_{j}") for j in range(SLOTS)]
        gelu_done = sem("gelu_done")
        coef_done = sem("coef_done")
        diag_done = [sem(f"diag_done_{j}") for j in range(SLOTS)]
        idx_rope = sem("index_rope_done")
        relu_read = sem("relu_read")
        index_scored = sem("index_scores_done")
        ret_rope = sem("retention_rope_done")
        ret_sq = sem("retention_squares")
        ret_ms = sem("retention_mean_square")
        ret_root = sem("retention_root")
        ret_done = sem("retention_head_done")
        att_rope = sem("attention_rope_done")
        att_bias = sem("attention_negative_max")
        att_exp = sem("attention_exp")
        att_probs = sem("attention_probs")
        stored = sem("stored")

        def vec(name, i):
            return vecs[:, VECS[name] + i:VECS[name] + i + 1]

        def vec_at(name, i, stride=1, shift=0):
            return vecs[:, bass.ds(i * stride + (VECS[name] + shift), 1)]

        def X(k):
            return xT[:, k, META:T2]

        FULL = ((0, S),)
        BLOCK2 = ((0, HALF), (HALF, HALF))

        totals = []
        block = ctx.enter_context(nc.Block())

        @block.sync
        def _(sp):
            for j in range(RING):
                sp.dma_start(slab[:, j, :], slabs_d[j]).then_inc(slab_landed[j], 16)
            turns = n_slabs // RING
            with sp.Fori(1, turns) as i:
                for j in range(RING):
                    sp.wait_ge(slab_used, i * RING + (j - RING + 2))
                    sp.dma_start(slab[:, j, :],
                                 slabs_d[bass.ds(i * RING + j, 1)].rearrange("o p n -> (o p) n"))\
                        .then_inc(slab_landed[j], 16)
            for n in range(turns * RING, n_slabs):
                sp.wait_ge(slab_used, n - RING + 2)
                sp.dma_start(slab[:, n % RING, :], slabs_d[n]).then_inc(slab_landed[n % RING], 16)
            sp.wait_ge(norm_out, KT * NORMS)
            sp.dma_start(out_d, nT[:, :, 0:S]).then_inc(stored, 16)
            sp.wait_ge(stored, 16)

        @block.tensor
        def _(pe):
            slabs, gm, at = Ring(RING), Ring(4), Ring(4, 4)
            norms = [0]

            def claim(ring):
                b, n = ring.take()
                pe.wait_ge(bank_free[b], n + 1)
                return b

            def drained(ring):
                for b, n in ring.taken():
                    if n:
                        pe.wait_ge(bank_free[b], n + 1)

            class Slab:

                def __init__(self):
                    self.slot, n = slabs.take()
                    pe.wait_ge(slab_landed[self.slot], n * 16 + 16)
                    self.told = False

                def tile(self, k):
                    return slab[:, self.slot, k * P:(k + 1) * P]

                def mm(self, out, lhsT, rhs, start, stop):
                    m = pe.matmul(out, lhsT, rhs, start=start, stop=stop)
                    if not self.told:
                        m.then_inc(slab_used, 1)
                        self.told = True
                    return m

            def product(rhs, parts=FULL, off=0):
                w = Slab()
                for a, n in parts:
                    b = claim(gm)
                    for k in range(KT):
                        m = w.mm(psum[:, b, 0:n], w.tile(k), rhs[:, k, off + a:off + a + n], k == 0, k == KT - 1)
                    m.then_inc(bank_full[b], 1)

            def product_k(rhs, off, meta, col):
                w = Slab()
                for k in range(KT):
                    m = w.mm(psum[:, meta, col:col + META], w.tile(k), rhs[:, k, 0:META], k == 0, k == KT - 1)
                b = claim(gm)
                for k in range(KT):
                    m2 = w.mm(psum[:, b, :], w.tile(k), rhs[:, k, META:T2], k == 0, k == KT - 1)
                m2.then_inc(bank_full[b], 1)
                return m

            def product_rows(lhs, tiles, off=0, meta=None, col=0):
                w = Slab()
                m = None
                if meta is not None:
                    for k in range(KT):
                        m = w.mm(psum[0:META, meta, col:col + P], lhs[:, k, 0:META], w.tile(k), k == 0, k == KT - 1)
                b = claim(gm)
                for tt in range(tiles):
                    for k in range(KT):
                        m2 = w.mm(psum[:, b, tt * P:(tt + 1) * P], lhs[:, k, off + tt * P:off + (tt + 1) * P],
                                  w.tile(k), k == 0, k == KT - 1)
                m2.then_inc(bank_full[b], 1)
                return m

            def column_sums(src, parts, ready, base, off=0):
                for h, (a, n) in enumerate(parts):
                    b = claim(at)
                    for k in range(KT):
                        if h == 0:
                            pe.wait_ge(ready, base + k + 1)
                        m = pe.matmul(psum[:, b, 0:n], ones[:, :], src[:, k, off + a:off + a + n],
                                      start=k == 0, stop=k == KT - 1)
                    m.then_inc(bank_full[b], 1)

            def norm(parts=FULL):
                column_sums(sq, parts, norm_sq, KT * norms[0])
                pe.wait_ge(norm_out, KT * (norms[0] + 1))
                norms[0] += 1

            for b in range(8):
                pe.sem_inc(bank_free[b], 1)
            pe.wait_ge(loaded, 16 * 6)
            norm()
            with repeat(pe, 2, [(slabs, 20), (gm, 20)]):
                for c in range(4):
                    for _ in range(5):
                        product(nT)
            column_sums(cfc, FULL, cf_done, 0)
            column_sums(sq, FULL, norm_sq, KT * norms[0])
            norms[0] += 1
            drained(gm)
            pe.wait_ge(cf_silu, KT)
            with repeat(pe, 4, [(slabs, 8), (gm, 8)]):
                for _ in range(2):
                    product(nT)
                    product(scy)
                    product(nT)
                    product(cfs)
            pe.wait_ge(merged_done, KT + 1)
            with repeat(pe, 2, [(slabs, 4), (gm, 4)]):
                for _ in range(4):
                    product(merged)

            norm(((0, MEM),))
            norm()

            def peek(ring, back):
                now = ring.base + ring.k - back
                n = now // ring.n + 1
                if ring.i is not None:
                    n = ring.i * (ring.per // ring.n) + n
                return ring.first + now % ring.n, n

            with repeat(pe, 2, [(slabs, 12), (gm, 12), (at, 20)]) as i:
                for h in range(2):
                    for _ in range(XA_DT):
                        product(memN, ((0, MEM),))
                    for _ in range(2):
                        product_rows(memN, MT)
                    for _ in range(XA_DT):
                        product(nT)
                    for back in range(6, 0, -1):
                        b, n = peek(gm, back)
                        pe.wait_ge(bank_free[b], n + 1)
                    for j in range(QT):
                        b = claim(at)
                        for d in range(XA_DT):
                            m = pe.matmul(psum[:, b, 0:MEM], xq[:, h, d * S + j * P:d * S + (j + 1) * P],
                                          xk[:, h, d * MEM:(d + 1) * MEM], start=d == 0, stop=d == XA_DT - 1)
                        m.then_inc(bank_full[b], 1)
                    for j in range(QT):
                        pe.wait_ge(xa_probs, i * (2 * QT) + (h * QT + j + 1))
                        b = claim(at)
                        for t in range(MT):
                            m = pe.transpose(psum[:, b, t * P:(t + 1) * P],
                                             xp[:, h, j * MEM + t * P:j * MEM + (t + 1) * P], ident[:, :])
                        m.then_inc(bank_full[b], 1)
                    for back in range(4, 0, -1):
                        b, n = peek(at, back)
                        pe.wait_ge(bank_free[b], n + 1)
                    for e in range(XA_DT):
                        b = claim(at)
                        for t in range(MT):
                            m = pe.matmul(psum[:, b, :], xv[:, h, t * 256 + e * P:t * 256 + (e + 1) * P],
                                          xpt[:, h, t * S:(t + 1) * S], start=t == 0, stop=t == MT - 1)
                        m.then_inc(bank_full[b], 1)
            drained(at)
            with repeat(pe, 2, [(slabs, 4), (gm, 4)]):
                for _ in range(4):
                    product(oT)

            norm()
            pe.wait_ge(subk_loaded, 16)

            def subscores(j):
                b, n = peek(gm, 1)
                pe.wait_ge(bank_free[b], n + 1)
                b = claim(at)
                for tt in range(QT):
                    m = pe.matmul(psum[:, b, tt * P:(tt + 1) * P], pq[:, j, tt * P:(tt + 1) * P],
                                  subk[:, j % 2, :], start=True, stop=True)
                m.then_inc(bank_full[b], 1)

            with repeat(pe, 4, [(slabs, 4), (gm, 4), (at, 4)]):
                for j in range(4):
                    product(nT)
                    subscores(j)
            for tt in range(QT):
                for q in range(2):
                    b = claim(at)
                    for k in range(4):
                        m = pe.transpose(psum[:, b, k * P:(k + 1) * P], nT[:, 4 * q + k, tt * P:(tt + 1) * P],
                                         ident[:, :])
                    m.then_inc(bank_full[b], 1)
            for tt in range(QT):
                banks, frees = [], []
                for q in range(2):
                    banks.append(claim(at))
                    frees.append(peek(at, 1))
                for q in range(2):
                    pe.matmul(psum[:, banks[q], :], zeros[:, 0:P], zeros[:, :], start=True, stop=False)
                with pe.Fori(tt * (PICKS // SLOTS), (tt + 1) * (PICKS // SLOTS)) as i:
                    for j in range(SLOTS):
                        pe.wait_ge(diag_done[j], i + 1)
                        pe.wait_ge(v_landed[j], i * 16 + 16)
                        for q in range(2):
                            m = pe.matmul(psum[:, banks[q], :], diag[:, j, :], v_rows[:, j, q * 512:(q + 1) * 512],
                                          start=False, stop=False)
                        m.then_inc(v_used[j], 1)
                for q in range(2):
                    pe.matmul(psum[:, banks[q], :], zeros[:, 0:P], zeros[:, :], start=False, stop=True)\
                        .then_inc(bank_full[banks[q]], 1)
                for q in range(2):
                    pe.wait_ge(bank_free[frees[q][0]], frees[q][1] + 1)
                    b = claim(at)
                    for k in range(4):
                        m = pe.transpose(psum[:, b, k * P:(k + 1) * P],
                                         out_rows[:, (4 * q + k) * P:(4 * q + k + 1) * P], ident[:, :])
                    m.then_inc(bank_full[b], 1)
            norm()

            def swiglu(parts, off):
                norm(parts)
                with repeat(pe, FT // 2, [(slabs, 4), (gm, 4 * len(parts))]):
                    for _ in range(2):
                        product(nT, parts)
                        product(nT, parts)
                drained(gm)
                with repeat(pe, 2, [(slabs, 12), (gm, 4 * len(parts))]):
                    for _ in range(4):
                        banks = [claim(gm) for _ in parts]
                        for s, nk in enumerate((8, 8, 6)):
                            w = Slab()
                            for b, (a, n) in zip(banks, parts):
                                for k in range(nk):
                                    f = 8 * s + k
                                    m = w.mm(psum[:, b, 0:n], w.tile(k), hid[:, f, a:a + n], f == 0, f == FT - 1)
                                if s == 2:
                                    m.then_inc(bank_full[b], 1)

            swiglu(BLOCK2, 0)

            norm(BLOCK2)
            for _ in range(4):
                product(nT, FULL, META)
            product(nT, FULL, META)
            pe.wait_ge(mixer_loaded, 16 * 7)
            b = claim(at)
            for tt in range(QT):
                for k in range(KT):
                    m = pe.matmul(psum[:, b, tt * 8:tt * 8 + 8], nT[:, k, META + tt * P:META + (tt + 1) * P],
                                  wi[:, k, :], start=k == 0, stop=k == KT - 1)
            m.then_inc(bank_full[b], 1)
            pe.wait_ge(idx_rope, 5)
            for j in range(1, QT):
                for h in range(IDX_HEADS):
                    b = claim(at)
                    r = 64 * (h % 2)
                    pe.matmul(psum[:, b, 0:(j + 1) * P], iq[r:r + 64, h // 2, j * P:(j + 1) * P],
                              ik[r:r + 64, 0:(j + 1) * P], start=True, stop=True).then_inc(bank_full[b], 1)
            drained(gm)

            pe.wait_ge(decay_loaded, 32)
            with repeat(pe, RET_HEADS, [(slabs, 12), (gm, 12), (at, 12)]) as i:
                for _ in range(2):
                    product(nT, FULL, META)
                km = claim(at)
                for d in range(2):
                    m = product_k(nT, META, km, d * META)
                m.then_inc(bank_full[km], 1)
                vm = claim(at)
                for e in range(4):
                    m = product_rows(nT, QT, META, vm, e * P)
                m.then_inc(bank_full[vm], 1)
                for _ in range(4):
                    product(nT, FULL, META)
                pe.wait_ge(ret_rope, i * 3 + 3)
                b = claim(at)
                for d in range(2):
                    m = pe.matmul(psum[0:META, b, :], rkm[:, d, :], rq[:, d, :], start=d == 0, stop=d == 1)
                m.then_inc(bank_full[b], 1)
                for s in range(QT):
                    b = claim(at)
                    for d in range(2):
                        m = pe.matmul(psum[:, b, 0:S - s * P], rk[:, d, s * P:(s + 1) * P], rq[:, d, s * P:S],
                                      start=d == 0, stop=d == 1)
                    m.then_inc(bank_full[b], 1)
                for back in range(8, 4, -1):
                    b, n = peek(gm, back)
                    pe.wait_ge(bank_free[b], n + 1)
                b, n = peek(at, 6)
                pe.wait_ge(bank_free[b], n + 1)
                for back in range(5, 0, -1):
                    b, n = peek(at, back)
                    pe.wait_ge(bank_free[b], n + 1)
                for e in range(4):
                    b = claim(at)
                    pe.matmul(psum[:, b, :], rvm[:, e * P:(e + 1) * P], rpm[:, :], start=True, stop=False)
                    for s in range(QT):
                        m = pe.matmul(psum[:, b, s * P:S], rv[:, s, e * P:(e + 1) * P], rp[:, s, s * P:S],
                                      start=False, stop=s == QT - 1)
                    m.then_inc(bank_full[b], 1)
                b = claim(at)
                for e in range(4):
                    pe.wait_ge(ret_sq, i * 4 + (e + 1))
                    m = pe.matmul(psum[:, b, :], ones[:, :], rsq[:, e, 0:S], start=e == 0, stop=e == 3)
                m.then_inc(bank_full[b], 1)
            pe.wait_ge(ret_done, 4 * RET_HEADS)
            with repeat(pe, 2, [(slabs, 12), (gm, 8)]):
                for _ in range(4):
                    product(nT, FULL, META)
                    b = claim(gm)
                    for s in range(2):
                        w = Slab()
                        for k in range(KT):
                            m = w.mm(psum[:, b, :], w.tile(k), yr[:, 8 * s + k, :], s + k == 0, s == 1 and k == KT - 1)
                    m.then_inc(bank_full[b], 1)
            with repeat(pe, ATT_HEADS, [(slabs, 4), (gm, 4), (at, 12)]) as i:
                product(nT, FULL, META)
                kv = claim(at)
                m = product_k(nT, META, kv, 0)
                m = product_rows(nT, QT, META, kv, P)
                m.then_inc(bank_full[kv], 1)
                product(nT, FULL, META)
                pe.wait_ge(att_rope, i * 3 + 3)
                b = claim(at)
                for j in range(QT):
                    m = pe.matmul(psum[:, b, j * META:(j + 1) * META], aq[:, j * P:(j + 1) * P], ak[:, 0:META],
                                  start=True, stop=True)
                m.then_inc(bank_full[b], 1)
                for j in range(QT):
                    b = claim(at)
                    pe.matmul(psum[:, b, 0:(j + 1) * P], aq[:, j * P:(j + 1) * P], ak[:, META:META + (j + 1) * P],
                              start=True, stop=True).then_inc(bank_full[b], 1)
                for j in range(QT):
                    pe.wait_ge(att_probs, i * QT + (j + 1))
                    b = claim(at)
                    for s in range(j + 1):
                        m = pe.transpose(psum[:, b, s * P:(s + 1) * P], ap_[:, j, META + s * P:META + (s + 1) * P],
                                         ident[:, :])
                    m.then_inc(bank_full[b], 1)
                b = claim(at)
                for j in range(QT):
                    m = pe.transpose(psum[0:META, b, j * P:(j + 1) * P], ap_[:, j, 0:META], ident[:, :])
                m.then_inc(bank_full[b], 1)
                b, n = peek(gm, 2)
                pe.wait_ge(bank_free[b], n + 1)
                for back in (11, 5, 4, 3, 2, 1):
                    b, n = peek(at, back)
                    pe.wait_ge(bank_free[b], n + 1)
                b = claim(at)
                pe.matmul(psum[:, b, :], avm[:, :], aptm[:, :], start=True, stop=False)
                for s in range(QT):
                    m = pe.matmul(psum[:, b, s * P:S], av[:, s, :], apt[:, s, s * P:S], start=False, stop=s == QT - 1)
                m.then_inc(bank_full[b], 1)
            drained(at)
            with repeat(pe, 2, [(slabs, 4), (gm, 4)]):
                for _ in range(4):
                    product(oT2)
            pe.wait_ge(merged_done, 2 * KT + 1)
            with repeat(pe, 2, [(slabs, 4), (gm, 4)]):
                for _ in range(4):
                    product(merged)
            swiglu(FULL, META)
            norm()
            totals.append((slabs.value(), gm.value(), at.value()))

        @block.scalar
        def _(act):
            gm, at = Ring(4), Ring(4, 4)
            norms = [0]

            def full(bn):
                act.wait_ge(bank_full[bn[0]], bn[1] + 1)
                return bn[0]

            def drained(ring):
                for b, n in ring.taken():
                    if n:
                        act.wait_ge(bank_free[b], n + 1)

            def norm(src, parts=FULL, off=0):
                T = parts[-1][0] + parts[-1][1]
                for k in range(KT):
                    act.activation(sq[:, k, 0:T], src[:, k, off:off + T], ACT.Square).then_inc(norm_sq, 1)
                for _ in parts:
                    at.take()
                act.wait_ge(norm_mean, norms[0] + 1)
                act.activation(norm_rs[:, 0:T], norm_ms[:, 0:T], ACT.Sqrt).then_inc(norm_root, 1)
                norms[0] += 1

            for k in range(0, KT, 2):
                act.dma_start(xT[:, k:k + 2, META:T2], xT_d[:, k:k + 2, :]).then_inc(loaded, 16)
            act.dma_start(vecs[:, :], vecs_d).then_inc(loaded, 16)
            act.dma_start(fixed[:, :], consts_d[:, 0:FIXED]).then_inc(loaded, 16)
            act.dma_start(xT[:, :, 0:META], metaT_d).then_inc(mem_loaded, 16)
            act.wait_ge(loaded, 16 * 6)
            norm(xT, off=META)

            with repeat(act, 2, [(gm, 20)]) as i:
                for c in range(4):
                    a, g, sc, sx, sb_ = (gm.take() for _ in range(5))
                    b = full(g)
                    act.activation(sg[:, c % 2, :], psum[:, b, :], ACT.Sigmoid, bias=vec_at("b1g", i, 4, c))\
                        .then_inc(bank_free[b], 1)
                    b = full(sx)
                    act.activation(xs[:, c % 2, :], psum[:, b, :], ACT.Copy).then_inc(bank_free[b], 1)
            at.take()
            act.wait_ge(cf_centred, KT)
            norm(cfc)
            for k in range(KT):
                act.wait_ge(norm_out, KT * (norms[0] - 1) + k + 1)
                act.activation(cfs[:, k, :], cfc[:, k, :], ACT.Silu, bias=vec("ln_b", k)).then_inc(cf_silu, 1)
            with repeat(act, 4, [(gm, 8)]):
                for c in range(2):
                    gsc, ysc, gcf, ycf = (gm.take() for _ in range(4))
                    b = full(gsc)
                    act.activation(sg[:, c, :], psum[:, b, :], ACT.Sigmoid).then_inc(bank_free[b], 1)
                    b = full(gcf)
                    act.activation(xs[:, c, :], psum[:, b, :], ACT.Sigmoid).then_inc(bank_free[b], 1)
            act.wait_ge(merged_done, KT + 1)
            act.dma_start(memT, memT_d).then_inc(mem_loaded, 16)
            for _ in range(8):
                gm.take()
            act.wait_ge(mem_loaded, 32)
            norm(memT, ((0, MEM),))
            drained(gm)
            norm(xT, off=META)

            with repeat(act, 2, [(gm, 12), (at, 20)]) as i:
                for h in range(2):
                    ks, vs, qs = ([gm.take() for _ in range(2)] for _ in range(3))
                    for d in range(XA_DT):
                        b = full(ks[d])
                        act.activation(xk[:, h, d * MEM:(d + 1) * MEM], psum[:, b, 0:MEM], ACT.Copy)\
                            .then_inc(bank_free[b], 1)
                    for d in range(XA_DT):
                        b = full(qs[d])
                        act.activation(xq[:, h, d * S:(d + 1) * S], psum[:, b, :], ACT.Copy)\
                            .then_inc(bank_free[b], 1)
                    for j in range(QT):
                        b = at.take()[0]
                        act.wait_ge(xa_bias, i * (2 * QT) + (h * QT + j + 1))
                        act.activation(xp[:, h, j * MEM:(j + 1) * MEM], psum[:, b, 0:MEM], ACT.Exp,
                                       bias=xneg[:, h, j:j + 1], scale=XA_SCALE, accum_out=xsum[:, h, j:j + 1])\
                            .then_inc(bank_free[b], 1)
                    for j in range(QT):
                        b = full(at.take())
                        act.activation(xpt[:, h, :].rearrange("p (t q) -> p t q", t=MT)[:, :, j * P:(j + 1) * P],
                                       psum[:, b, 0:MEM].rearrange("p (t q) -> p t q", t=MT), ACT.Copy)\
                            .then_inc(bank_free[b], 1)
                    for e in range(XA_DT):
                        b = full(at.take())
                        act.activation(row(oT, i * 4 + (2 * h + e), 0, S), psum[:, b, :], ACT.Copy)\
                            .then_inc(bank_free[b], 1)
            for _ in range(8):
                gm.take()
            drained(gm)
            act.dma_start(subk, subk_d).then_inc(subk_loaded, 16)
            norm(xT, off=META)
            with repeat(act, 4, [(gm, 4), (at, 4)]):
                for j in range(4):
                    b = full(gm.take())
                    act.activation(pq[:, j, :], psum[:, b, :], ACT.Copy).then_inc(bank_free[b], 1)
                    at.take()
            for tt in range(QT):
                for q in range(2):
                    b = full(at.take())
                    act.activation(hrow[:, tt, q * 512:(q + 1) * 512], psum[:, b, :], ACT.Copy)\
                        .then_inc(bank_free[b], 1)

            def gate_exps(tt):
                act.wait_ge(gate_in, tt + 1)
                act.activation(fin_e, fin_bf, ACT.Exp).then_inc(gate_exp, 1)

            gate_exps(0)
            turns = PICKS // TURN
            for tt in range(QT):
                banks = [at.take(), at.take()]
                for quarter in range(4):
                    if quarter == 2 and tt + 1 < QT:
                        gate_exps(tt + 1)
                    first = tt * turns + quarter * turns // 4
                    with act.Fori(first, first + turns // 4) as i:
                        for g in range(4):
                            slots = [g % 2 * GROUP + j for j in range(GROUP)]
                            act.wait_ge(u_used[slots[-1]], i * 2 + (g // 2 + 2))
                            act.activation(acts[:, g, :], dots[:, g, :], ACT.Gelu).then_inc(gelu_done, 1)
                            act.wait_ge(coef_done, i * 4 + (g + 1))
                            for j, slot in enumerate(slots):
                                act.wait_ge(v_used[slot], i * 2 + (g // 2 + 1))
                                act.activation(diag[:, slot, :], ident[:, :], ACT.Copy, scale=coefs[:, g, j:j + 1])\
                                    .then_inc(diag_done[slot], 1)
                for q in range(2):
                    b = full(banks[q])
                    if tt:
                        pb, pn = before[q]
                        act.wait_ge(bank_full[pb], pn + 1)
                    act.activation(out_rows[:, q * 512:(q + 1) * 512], psum[:, b, :], ACT.Copy)\
                        .then_inc(bank_free[b], 1)
                before = [at.take(), at.take()]
            drained(at)
            norm(xT, off=META)
            act.wait_ge(norm_out, KT * norms[0])

            def swiglu(parts, off):
                T = parts[-1][0] + parts[-1][1]
                norm(xT, parts, off)
                with repeat(act, FT // 2, [(gm, 4 * len(parts))]):
                    for c in range(2):
                        for _ in parts:
                            gm.take()
                        for a, n in parts:
                            b = full(gm.take())
                            act.activation(silu[:, c, a:a + n], psum[:, b, 0:n], ACT.Silu)\
                                .then_inc(bank_free[b], 1)
                for _ in range(8 * len(parts)):
                    gm.take()
                drained(gm)

            swiglu(BLOCK2, 0)
            for v, a in zip((cos_r, sin_r, cos_a, sin_a, cos_i, sin_i), range(0, 6 * T2, T2)):
                act.dma_start(v, consts_d[:, TABLES + a:TABLES + a + T2]).then_inc(mixer_loaded, 16)
            act.dma_start(wi, wi_d).then_inc(mixer_loaded, 16)
            norm(xT, BLOCK2)
            for _ in range(5):
                gm.take()
            at.take()
            for j in range(1, QT):
                for h in range(IDX_HEADS):
                    n = (j - 1) * IDX_HEADS + h
                    b = full(at.take())
                    if n >= 2:
                        act.wait_ge(relu_read, n - 1)
                    act.activation(relu[:, h % 2, 0:(j + 1) * P], psum[:, b, 0:(j + 1) * P], ACT.Relu)\
                        .then_inc(bank_free[b], 1)
            act.wait_ge(index_scored, 1)
            act.dma_start(decay, consts_d[:, DECAY:DECAY + RET_HEADS * S].rearrange("p (h n) -> p h n", h=RET_HEADS))\
                .then_inc(decay_loaded, 16)
            act.dma_start(decay_m, consts16_d.rearrange("p (h n) -> p h n", h=RET_HEADS)).then_inc(decay_loaded, 16)
            with repeat(act, RET_HEADS, [(gm, 12), (at, 12)]) as i:
                for _ in range(4):
                    gm.take()
                at.take()
                vm = at.take()
                for e in range(4):
                    b = full(gm.take())
                    act.activation(rv[:, :, e * P:(e + 1) * P], psum[:, b, :].rearrange("p (t n) -> p t n", t=QT),
                                   ACT.Copy).then_inc(bank_free[b], 1)
                b = full(vm)
                act.activation(rvm, psum[0:META, b, :], ACT.Copy).then_inc(bank_free[b], 1)
                for e in range(4):
                    b = full(gm.take())
                    act.activation(rg[:, e, :], psum[:, b, :], ACT.Silu).then_inc(bank_free[b], 1)
                for _ in range(5):
                    at.take()
                ys = []
                for e in range(4):
                    ys.append(at.take())
                    b = full(ys[-1])
                    act.activation(ry[:, e, :], psum[:, b, :], ACT.Copy).then_inc(bank_free[b], 1)
                for e in range(4):
                    b, n = ys[e]
                    act.wait_ge(bank_free[b], n + 2)
                    act.activation(rsq[:, e, 0:S], ry[:, e, :], ACT.Square).then_inc(ret_sq, 1)
                at.take()
                act.wait_ge(ret_ms, i + 1)
                act.activation(norm_rs[:, 0:S], norm_ms[:, 0:S], ACT.Sqrt).then_inc(ret_root, 1)
            act.wait_ge(ret_done, 4 * RET_HEADS)
            with repeat(act, 2, [(gm, 8)]):
                for c in range(4):
                    b = full(gm.take())
                    act.activation(gs[:, c, :], psum[:, b, :], ACT.Sigmoid).then_inc(bank_free[b], 1)
                    gm.take()
            with repeat(act, ATT_HEADS, [(gm, 4), (at, 12)]) as i:
                gm.take()
                kv = at.take()
                gm.take()
                v, g = gm.take(), gm.take()
                b = full(v)
                act.activation(av[:, :, :], psum[:, b, :].rearrange("p (t n) -> p t n", t=QT), ACT.Copy)\
                    .then_inc(bank_free[b], 1)
                b = full(g)
                act.activation(row(sga, i, 0, S), psum[:, b, :], ACT.Sigmoid).then_inc(bank_free[b], 1)
                act.wait_ge(att_rope, i * 3 + 3)
                act.activation(avm, psum[0:META, kv[0], P:2 * P], ACT.Copy).then_inc(bank_free[kv[0]], 1)
                at.take()
                for j in range(QT):
                    at.take()
                    act.wait_ge(att_bias, i * QT + (j + 1))
                    act.activation(ap_[:, j, 0:META + (j + 1) * P], ap_[:, j, 0:META + (j + 1) * P], ACT.Exp,
                                   bias=aneg[:, j:j + 1], accum_out=asum[:, j:j + 1]).then_inc(att_exp, 1)
                for j in range(QT):
                    b = full(at.take())
                    act.activation(apt[:, 0:j + 1, j * P:(j + 1) * P],
                                   psum[:, b, 0:(j + 1) * P].rearrange("p (t n) -> p t n", t=j + 1), ACT.Copy)\
                        .then_inc(bank_free[b], 1)
                b = full(at.take())
                act.activation(aptm, psum[0:META, b, :], ACT.Copy).then_inc(bank_free[b], 1)
                b = full(at.take())
                act.activation(row(oT2, i, 0, S), psum[:, b, :], ACT.Copy).then_inc(bank_free[b], 1)
            for _ in range(8 + 8):
                gm.take()
            drained(gm)
            swiglu(FULL, META)
            norm(xT, off=META)
            totals.append((gm.value(), at.value()))

        @block.vector
        def _(dve):
            gm, at = Ring(4), Ring(4, 4)
            chain = Chain(dve, dve_step)
            step, sync = chain.step, chain.wait
            norms = [0]

            def sync_apart():
                sync()
                dve.sem_inc(dve_passed, 1)

            def full(bn):
                dve.wait_ge(bank_full[bn[0]], bn[1] + 1)
                return bn[0]

            def norm(src, dst, gain, parts=FULL, off=0, dst_off=0):
                T = parts[-1][0] + parts[-1][1]
                dve.wait_ge(norm_out, KT * norms[0])
                for a, n in parts:
                    b = full(at.take())
                    m = dve.tensor_scalar(norm_ms[:, a:a + n], psum[:, b, 0:n], 1.0 / D, EPS, ALU.mult, ALU.add)
                    m.then_inc(bank_free[b], 1)
                drained(at)
                dve.sem_inc(norm_mean, 1)
                dve.wait_ge(norm_root, norms[0] + 1)
                step(dve.reciprocal(norm_ms[:, 0:T], norm_rs[:, 0:T]))
                sync()
                for k in range(KT):
                    dve.scalar_tensor_tensor(out=dst[:, k, dst_off:dst_off + T], in0=src[:, k, off:off + T],
                                             scalar=vec(gain, k), in1=norm_ms[:, 0:T], op0=ALU.mult, op1=ALU.mult)\
                        .then_inc(norm_out, 1)
                norms[0] += 1

            def add_to_stream(n_turns):
                with repeat(dve, n_turns, [(gm, 4)]) as i:
                    for c in range(4):
                        b = full(gm.take())
                        x = row(xT, i * 4 + c, META, T2)
                        dve.tensor_tensor(x, psum[:, b, :], x, ALU.add).then_inc(bank_free[b], 1)

            def drained(ring):
                for b, n in ring.taken():
                    if n:
                        dve.wait_ge(bank_free[b], n + 1)

            dve.sem_inc(merged_done, 1)
            step(dve.memset(cfp[:, :, 0:CF_K - 1], 0.0))
            step(dve.memset(scp[:, :, 0:SC_K - 1], 0.0))
            step(dve.memset(zeros[:, :], 0.0))
            sync()
            dve.wait_ge(loaded, 16 * 6)
            norm(xT, nT, "norm_mix", off=META)

            with repeat(dve, 2, [(gm, 20), (chain, 4 * 35)]) as i:
                for c in range(4):
                    a, g, sc, sx, sb_ = (gm.take() for _ in range(5))
                    h = c % 2
                    b = full(a)
                    dve.wait_ge(bank_free[g[0]], g[1] + 2)
                    dve.scalar_tensor_tensor(out=cfp[:, h, CF_K - 1:], in0=psum[:, b, :], scalar=vec_at("b1a", i, 4, c),
                                             in1=sg[:, h, :], op0=ALU.add, op1=ALU.mult).then_inc(bank_free[b], 1)
                    b = full(sc)
                    dve.wait_ge(bank_free[sx[0]], sx[1] + 2)
                    dve.tensor_tensor(scp[:, h, SC_K - 1:], psum[:, b, :], xs[:, h, :], ALU.mult)\
                        .then_inc(bank_free[b], 1)
                    dve.wait_ge(bank_free[b], sc[1] + 2)
                    for t in range(SC_K):
                        w = vec_at("sc_w", i, 4 * SC_K, c * SC_K + t)
                        if t == 0:
                            step(dve.tensor_scalar(sct[:, h, :], scp[:, h, 0:S], w, None, ALU.mult))
                        else:
                            step(dve.scalar_tensor_tensor(out=sct[:, h, :], in0=scp[:, h, t:t + S], scalar=w,
                                                          in1=sct[:, h, :], op0=ALU.mult, op1=ALU.add))
                        sync()
                    b = full(sb_)
                    dve.tensor_tensor(row(scy, i * 4 + c, 0, S), psum[:, b, :], sct[:, h, :], ALU.mult)\
                        .then_inc(bank_free[b], 1)
                    dve.wait_ge(bank_free[a[0]], a[1] + 2)
                    for t in range(CF_K):
                        acc = acc_o if t % 2 else acc_e
                        w = vec_at("cf_w", i, 4 * CF_K, c * CF_K + t)
                        if t > 1:
                            sync(1)
                        if t < 2:
                            step(dve.tensor_scalar(acc, cfp[:, h, t:t + S], w, None, ALU.mult))
                        else:
                            step(dve.scalar_tensor_tensor(out=acc, in0=cfp[:, h, t:t + S], scalar=w, in1=acc,
                                                          op0=ALU.mult, op1=ALU.add))
                    sync()
                    step(dve.scalar_tensor_tensor(out=row(cfc, i * 4 + c, 0, S), in0=acc_e,
                                                  scalar=vec_at("cf_b", i, 4, c), in1=acc_o, op0=ALU.add, op1=ALU.add))
                    sync()
                    dve.sem_inc(cf_done, 1)
            bn = at.take()
            b = full(bn)
            dve.tensor_scalar(mu, psum[:, b, :], 1.0 / D, None, ALU.mult).then_inc(bank_free[b], 1)
            dve.wait_ge(bank_free[b], bn[1] + 2)
            for k in range(KT):
                dve.tensor_tensor(cfc[:, k, :], cfc[:, k, :], mu, ALU.subtract).then_inc(cf_centred, 1)
            dve.wait_ge(cf_centred, KT)
            norm(cfc, cfc, "ln_g")
            with repeat(dve, 4, [(gm, 8)]) as i:
                for c in range(2):
                    gsc, ysc, gcf, ycf = (gm.take() for _ in range(4))
                    b = full(ysc)
                    dve.wait_ge(bank_free[gsc[0]], gsc[1] + 2)
                    dve.wait_ge(merged_done, i * 2 + (c + 1))
                    dve.tensor_tensor(acc_e, psum[:, b, :], sg[:, c, :], ALU.mult).then_inc(bank_free[b], 1)
                    b2 = full(ycf)
                    dve.wait_ge(bank_free[gcf[0]], gcf[1] + 2)
                    dve.scalar_tensor_tensor(out=acc_o, in0=psum[:, b2, :], scalar=vec_at("pw2_b", i, 2, c),
                                             in1=xs[:, c, :], op0=ALU.add, op1=ALU.mult).then_inc(bank_free[b2], 1)
                    dve.wait_ge(bank_free[b], ysc[1] + 2)
                    dve.wait_ge(bank_free[b2], ycf[1] + 2)
                    dve.tensor_tensor(row(merged, i * 2 + c, 0, S), acc_e, acc_o, ALU.add).then_inc(merged_done, 1)
            add_to_stream(2)

            norm(memT, memN, "norm_mem", ((0, MEM),))
            drained(gm)
            norm(xT, nT, "norm_xa", off=META)
            with repeat(dve, 2, [(gm, 12), (at, 20), (chain, 4 * QT)]) as i:
                for h in range(2):
                    ks, vs, qs = ([gm.take() for _ in range(2)] for _ in range(3))
                    for e in range(2):
                        b = full(vs[e])
                        dve.tensor_copy(xv[:, h, :].rearrange("p (t n) -> p t n", t=MT)[:, :, e * P:(e + 1) * P],
                                        psum[:, b, 0:MEM].rearrange("p (t n) -> p t n", t=MT))\
                            .then_inc(bank_free[b], 1)
                    scores = [at.take() for _ in range(QT)]
                    for j in range(QT):
                        b = full(scores[j])
                        step(dve.reduce_max(xmax[:, h, j:j + 1], psum[:, b, 0:MEM], AX))
                        sync()
                        dve.tensor_scalar(xneg[:, h, j:j + 1], xmax[:, h, j:j + 1], -XA_SCALE, None, ALU.mult)\
                            .then_inc(xa_bias, 1)
                    for j in range(QT):
                        b, n = scores[j]
                        dve.wait_ge(bank_free[b], n + 2)
                        step(dve.reciprocal(xinv[:, h, j:j + 1], xsum[:, h, j:j + 1]))
                        sync()
                        dve.tensor_scalar(xp[:, h, j * MEM:(j + 1) * MEM], xp[:, h, j * MEM:(j + 1) * MEM],
                                          xinv[:, h, j:j + 1], None, ALU.mult).then_inc(xa_probs, 1)
                    for _ in range(QT + XA_DT):
                        at.take()
            add_to_stream(2)
            drained(gm)
            norm(xT, nT, "norm_peer", off=META)

            with repeat(dve, 4, [(gm, 4), (at, 4)]) as i:
                for j in range(4):
                    gm.take()
                    b = full(at.take())
                    dve.tensor_copy(sub_s[:, bass.ds(i * (4 * QT) + j * QT, QT), :],
                                    psum[:, b, :].rearrange("p (t n) -> p t n", t=QT)).then_inc(bank_free[b], 1)
            drained(at)
            for _ in range(2 * QT):
                at.take()
            B2 = 2 * PEER_HEADS
            by_tile = sub_s.rearrange("p (b t) n -> p t b n", t=QT)
            ids = tk_f.rearrange("p (h s) k -> p h s k", s=2)
            halves = tk_v.rearrange("p (h s) k -> p h s k", s=2)
            hot = onehot.rearrange("p (h k) n -> p h k n", h=PEER_HEADS)
            four = [P, PEER_HEADS, TOPK, TOPK]

            def keep_first(tt):
                step(dve.tensor_copy(tk_in, by_tile[:, tt]))
                sync()
                for q in range(B2):
                    step(dve.max(tk_v[:, q, 0:8], tk_in[:, q, :]))
                sync()
                for q in range(B2):
                    step(dve.max_index(tk_i[:, q, 0:8], tk_v[:, q, 0:8], tk_in[:, q, :]))
                    step(dve.match_replace(tk_wk[:, q, :], tk_v[:, q, 0:8], tk_in[:, q, :], FLOOR))
                sync()

            def keep_second(tt):
                for q in range(B2):
                    step(dve.max(tk_v[:, q, 8:16], tk_wk[:, q, :]))
                sync()
                for q in range(B2):
                    step(dve.max_index(tk_i[:, q, 8:16], tk_v[:, q, 8:16], tk_wk[:, q, :]))
                step(dve.tensor_tensor(cand.rearrange("p h (a b) -> p h a b", a=TOPK),
                                       halves[:, :, 0, :].unsqueeze(3).to_broadcast(four),
                                       halves[:, :, 1, :].unsqueeze(2).to_broadcast(four), ALU.add))
                sync()
                step(dve.tensor_copy(tk_f, tk_i))

            def keep_sums(tt):
                for h in range(PEER_HEADS):
                    step(dve.max(fin_v[:, h, 0:8], cand[:, h, :]))
                sync()
                for h in range(PEER_HEADS):
                    step(dve.max_index(fin_p[:, h, 0:8], fin_v[:, h, 0:8], cand[:, h, :]))
                    step(dve.match_replace(cand_wk[:, h, :], fin_v[:, h, 0:8], cand[:, h, :], FLOOR))
                sync()
                for h in range(PEER_HEADS):
                    step(dve.max(fin_v[:, h, 8:16], cand_wk[:, h, :]))
                sync()
                for h in range(PEER_HEADS):
                    step(dve.max_index(fin_p[:, h, 8:16], fin_v[:, h, 8:16], cand_wk[:, h, :]))
                step(dve.tensor_tensor(fin_bf, fin_v, fin_v[:, :, 0:1].to_broadcast([P, PEER_HEADS, TOPK]),
                                       ALU.subtract))
                sync()
                dve.sem_inc(gate_in, 1)
                dve.wait_ge(gate_exp, tt + 1)
                step(dve.reduce_sum(fin_s, fin_e, AX))
                sync()
                step(dve.reciprocal(fin_r, fin_s))
                sync()
                step(dve.tensor_tensor(gates[:, tt, :].rearrange("p (h k) -> p h k", h=PEER_HEADS),
                                       fin_e, fin_r.unsqueeze(2).to_broadcast([P, PEER_HEADS, TOPK]), ALU.mult))

            def name_experts(tt):
                step(dve.tensor_scalar(fin_a, fin_p, 4, None, ALU.logical_shift_right))
                step(dve.tensor_scalar(fin_b, fin_p, 15, None, ALU.bitwise_and))
                sync()
                step(dve.tensor_copy(fin_af, fin_a))
                step(dve.tensor_copy(fin_bf, fin_b))
                for s, (place, key) in enumerate(((fin_af, fin_i0), (fin_bf, fin_i1))):
                    sync()
                    step(dve.tensor_tensor(
                        onehot, iota16.unsqueeze(1).to_broadcast([P, PICKS, TOPK]),
                        place.rearrange("p a b -> p (a b)").unsqueeze(2).to_broadcast([P, PICKS, TOPK]), ALU.is_equal))
                    sync()
                    step(dve.tensor_tensor(hot, hot, ids[:, :, s, :].unsqueeze(2).to_broadcast(four), ALU.mult))
                    sync()
                    step(dve.reduce_sum(key.rearrange("p a b -> p (a b)"), onehot, AX))
                sync()
                step(dve.scalar_tensor_tensor(out=fin_af, in0=fin_i0, scalar=float(P), in1=fin_i1,
                                              op0=ALU.mult, op1=ALU.add))
                sync()
                step(dve.tensor_copy(eidx[:, tt, :], fin_af.rearrange("p a b -> p (a b)")))
                sync()
                dve.sem_inc(picked, 1)

            choice = (keep_first, keep_second, keep_sums, name_experts)
            for work_on in choice:
                work_on(0)
            drained(at)
            turns = PICKS // TURN
            for tt in range(QT):
                banks = [at.take(), at.take()]
                turned = [at.take(), at.take()]
                gate_groups = gates[:, tt, :].rearrange("p (g j) -> p g j", j=GROUP)
                for quarter in range(4):
                    if tt + 1 < QT:
                        choice[quarter](tt + 1)
                    first = tt * turns + quarter * turns // 4
                    with dve.Fori(first, first + turns // 4) as i:
                        for g in range(4):
                            for j in range(GROUP):
                                slot = g % 2 * GROUP + j
                                dve.wait_ge(u_landed[slot], i * 32 + (g // 2 * 16 + 16))
                                if slot:
                                    dve.wait_ge(u_used[slot - 1], i * 2 + (g // 2 + 2))
                                else:
                                    dve.wait_ge(u_used[SLOTS - 1], i * 2 + (g // 2 + 1))
                                dve.tensor_tensor_reduce(dump, u_rows[:, slot, :], hrow[:, tt, :], 1.0, 0.0, ALU.mult,
                                                         ALU.add, dots[:, g, j:j + 1]).then_inc(u_used[slot], 1)
                            dve.wait_ge(gelu_done, i * 4 + (g + 1))
                            dve.tensor_tensor(coefs[:, g, :], acts[:, g, :],
                                              gate_groups[:, bass.ds(i * 4 + (g - tt * turns * 4), 1), :]
                                              .rearrange("p a j -> p (a j)"), ALU.mult).then_inc(coef_done, 1)
                for q in range(2):
                    b = full(turned[q])
                    x = xT[:, 4 * q:4 * q + 4, META + tt * P:META + (tt + 1) * P]
                    dve.tensor_tensor(x, psum[:, b, :].rearrange("p (k n) -> p k n", k=4), x, ALU.add)\
                        .then_inc(bank_free[b], 1)
            norm(xT, xT, "final1", off=META, dst_off=META)
            dve.wait_ge(norm_out, KT * norms[0])

            def swiglu(gain, parts, off):
                norm(xT, nT, gain, parts, off)
                with repeat(dve, FT // 2, [(gm, 4 * len(parts))]) as i:
                    for c in range(2):
                        ups, gts = ([gm.take() for _ in parts] for _ in range(2))
                        for (a, n), u, g in zip(parts, ups, gts):
                            b = full(u)
                            dve.wait_ge(bank_free[g[0]], g[1] + 2)
                            dve.tensor_tensor(row(hid, i * 2 + c, a, a + n), psum[:, b, 0:n], silu[:, c, a:a + n],
                                              ALU.mult).then_inc(bank_free[b], 1)
                with repeat(dve, 2, [(gm, 4 * len(parts))]) as i:
                    for c in range(4):
                        for a, n in parts:
                            b = full(gm.take())
                            x = row(xT, i * 4 + c, off + a, off + a + n)
                            dve.scalar_tensor_tensor(out=x, in0=psum[:, b, 0:n], scalar=0.5, in1=x, op0=ALU.mult,
                                                     op1=ALU.add).then_inc(bank_free[b], 1)
                drained(gm)

            swiglu("ffn1", BLOCK2, 0)
            norm(xT, nT, "mix2", BLOCK2)
            dve.wait_ge(mixer_loaded, 16 * 7)

            def rope_blocks(dst, b, width, cos, sin, size, off, done_bank):
                t = rope_t[:, 0, 0:width]
                step(dve.tensor_tensor(dst, psum[:, b, 0:width], cos[:, off:off + width], ALU.mult))
                for r in range(0, P, size):
                    o = r + size if (r // size) % 2 == 0 else r - size
                    ins = dve.tensor_tensor(rope_t[o:o + size, 0, 0:width], psum[r:r + size, b, 0:width],
                                            sin[r:r + size, off:off + width], ALU.mult)
                    step(ins)
                sync()
                dve.sem_inc(bank_free[b], 1)
                step(dve.tensor_tensor(dst, dst, t, ALU.add))
                sync()

            for q in range(5):
                b = full(gm.take())
                rope_blocks(iq[:, q, :] if q < 4 else ik, b, S, cos_i, sin_i, 32, META, None)
                dve.sem_inc(idx_rope, 1)
            bn = at.take()
            b = full(bn)
            dve.tensor_copy(iw.rearrange("p t h -> p (t h)"), psum[:, b, 0:QT * IDX_HEADS]).then_inc(bank_free[b], 1)
            dve.wait_ge(bank_free[b], bn[1] + 2)
            for j in range(1, QT):
                w = (j + 1) * P
                for h in range(IDX_HEADS):
                    b, n = at.take()
                    dve.wait_ge(bank_free[b], n + 2)
                    if h == 0:
                        dve.tensor_scalar(score[:, j - 1, 0:w], relu[:, h % 2, 0:w], iw[:, j, h:h + 1], None,
                                          ALU.mult).then_inc(relu_read, 1)
                    else:
                        dve.wait_ge(relu_read, (j - 1) * IDX_HEADS + h)
                        dve.scalar_tensor_tensor(out=score[:, j - 1, 0:w], in0=relu[:, h % 2, 0:w],
                                                 scalar=iw[:, j, h:h + 1], in1=score[:, j - 1, 0:w],
                                                 op0=ALU.mult, op1=ALU.add).then_inc(relu_read, 1)
            dve.wait_ge(relu_read, 3 * IDX_HEADS)
            for j in range(1, QT):
                step(dve.tensor_scalar(work[:, j - 1, 0:(j + 1) * P], score[:, j - 1, 0:(j + 1) * P], IDX_SCALE, None,
                                       ALU.mult))
            sync()
            step(dve.tensor_scalar(relu[:, 0, 0:P], tri[:, :], -FAR, FAR, ALU.mult, ALU.add))
            sync()
            for j in range(1, QT):
                dg = work[:, j - 1, j * P:(j + 1) * P]
                step(dve.tensor_tensor(dg, dg, tri[:, :], ALU.mult))
            sync()
            for j in range(1, QT):
                dg = work[:, j - 1, j * P:(j + 1) * P]
                step(dve.tensor_tensor(dg, dg, relu[:, 0, 0:P], ALU.add))
            sync()
            dve.sem_inc(index_scored, 1)

            def keep_keys():
                for j in range(1, QT):
                    step(dve.max(top8[:, j - 1, :], work[:, j - 1, 0:(j + 1) * P]))
                sync_apart()
                for j in range(1, QT):
                    wk = work[:, j - 1, 0:(j + 1) * P]
                    step(dve.match_replace(wk, top8[:, j - 1, :], wk, TAKEN))
                sync_apart()

            dve.wait_ge(decay_loaded, 32)

            def rope_pair(dst, a, b, width, off, tmp):
                c, s = cos_r[:, off:off + width], sin_r[:, off:off + width]
                (pa, fa), (pb, fb) = a, b
                step(dve.tensor_tensor(tmp[:, 0, 0:width], pa, c, ALU.mult))
                step(dve.tensor_tensor(tmp[:, 3, 0:width], pa, s, ALU.mult))
                step(dve.tensor_tensor(tmp[:, 1, 0:width], pb, s, ALU.mult))
                step(dve.tensor_tensor(tmp[:, 2, 0:width], pb, c, ALU.mult))
                sync()
                for f in dict.fromkeys((fa, fb)):
                    dve.sem_inc(bank_free[f], 1)
                step(dve.tensor_tensor(dst[:, 0, :], tmp[:, 0, 0:width], tmp[:, 1, 0:width], ALU.subtract))
                step(dve.tensor_tensor(dst[:, 1, :], tmp[:, 2, 0:width], tmp[:, 3, 0:width], ALU.add))
                sync()
                dve.sem_inc(ret_rope, 1)

            with repeat(dve, RET_HEADS, [(gm, 12), (at, 12), (chain, 18 + 1 + 4 + 6 * (KEEP // 8 // RET_HEADS))]) as i:
                q = [gm.take() for _ in range(2)]
                k = [gm.take() for _ in range(2)]
                km, vm = at.take(), at.take()
                vg = [gm.take() for _ in range(8)]
                b0, b1 = full(q[0]), full(q[1])
                rope_pair(rq, (psum[:, b0, :], b0), (psum[:, b1, :], b1), S, META, rt)
                b0, b1 = full(k[0]), full(k[1])
                rope_pair(rk, (psum[:, b0, :], b0), (psum[:, b1, :], b1), S, META, rt)
                b = full(km)
                rope_pair(rkm, (psum[:, b, 0:META], b), (psum[:, b, META:2 * META], b), META, 0, rtm)
                for _ in range(KEEP // 8 // RET_HEADS):
                    keep_keys()
                b = full(at.take())
                dve.tensor_tensor(rpm, psum[0:META, b, :], row(decay_m, i, 0, S), ALU.mult).then_inc(bank_free[b], 1)
                for s in range(QT):
                    b = full(at.take())
                    dve.tensor_tensor(rp[:, s, s * P:S], psum[:, b, 0:S - s * P], row(decay, i, 0, S - s * P),
                                      ALU.mult).then_inc(bank_free[b], 1)
                ys = [at.take() for _ in range(4)]
                bn = at.take()
                b = full(bn)
                dve.tensor_scalar(norm_ms[:, 0:S], psum[:, b, :], 1.0 / RET_DV, EPS, ALU.mult, ALU.add)\
                    .then_inc(bank_free[b], 1)
                dve.wait_ge(bank_free[b], bn[1] + 2)
                dve.sem_inc(ret_ms, 1)
                dve.wait_ge(ret_root, i + 1)
                step(dve.reciprocal(norm_ms[:, 0:S], norm_rs[:, 0:S]))
                sync()
                for e in range(4):
                    step(dve.tensor_tensor(ry[:, e, :], ry[:, e, :], norm_ms[:, 0:S], ALU.mult))
                sync()
                for e in range(4):
                    b, n = vg[4 + e]
                    dve.wait_ge(bank_free[b], n + 2)
                    dve.tensor_tensor(row(yr, i * 4 + e, 0, S), ry[:, e, :], rg[:, e, :], ALU.mult)\
                        .then_inc(ret_done, 1)
            for j in range(1, QT):
                w = work[:, j - 1, 0:(j + 1) * P]
                step(dve.tensor_scalar(w, w, TAKEN, HIDE, ALU.not_equal, ALU.mult))
            step(dve.tensor_scalar(key_bias[:, 0, 0:P], tri[:, :], -HIDE, HIDE, ALU.mult, ALU.add))
            sync()
            with repeat(dve, 2, [(gm, 8)]) as i:
                for c in range(4):
                    g, y = gm.take(), gm.take()
                    b = full(y)
                    dve.wait_ge(bank_free[g[0]], g[1] + 2)
                    dve.tensor_tensor(row(merged, i * 4 + c, 0, S), psum[:, b, :], gs[:, c, :], ALU.mult)\
                        .then_inc(bank_free[b], 1)

            def rope_halves(dst, src, b, t, width, off, frees):
                step(dve.tensor_tensor(dst, src, cos_a[:, off:off + width], ALU.mult))
                step(dve.tensor_tensor(t[64:128], src[0:64], sin_a[0:64, off:off + width], ALU.mult))
                step(dve.tensor_tensor(t[0:64], src[64:128], sin_a[64:128, off:off + width], ALU.mult))
                sync()
                if frees:
                    dve.sem_inc(bank_free[b], 1)
                step(dve.tensor_tensor(dst, dst, t, ALU.add))
                sync()
                dve.sem_inc(att_rope, 1)

            with repeat(dve, ATT_HEADS, [(gm, 4), (at, 12), (chain, 12 + 3 * QT)]) as i:
                q, k, v, g = (gm.take() for _ in range(4))
                kv = at.take()
                b = full(q)
                rope_halves(aq, psum[:, b, :], b, at_t[:, 0, :], S, META, True)
                b = full(k)
                rope_halves(ak[:, META:T2], psum[:, b, :], b, at_t[:, 1, :], S, META, True)
                b = full(kv)
                rope_halves(ak[:, 0:META], psum[:, b, 0:META], b, at_tm, META, 0, False)
                mb = full(at.take())
                for j in range(QT):
                    step(dve.tensor_scalar(ap_[:, j, 0:META], psum[:, mb, j * META:(j + 1) * META], ATT_SCALE, None,
                                           ALU.mult))
                sync()
                dve.sem_inc(bank_free[mb], 1)
                for j in range(QT):
                    w = (j + 1) * P
                    bn = at.take()
                    b = full(bn)
                    dve.scalar_tensor_tensor(out=ap_[:, j, META:META + w], in0=psum[:, b, 0:w], scalar=ATT_SCALE,
                                             in1=key_bias[:, j, 0:w], op0=ALU.mult, op1=ALU.add)\
                        .then_inc(bank_free[b], 1)
                    dve.wait_ge(bank_free[b], bn[1] + 2)
                    step(dve.reduce_max(amax[:, j:j + 1], ap_[:, j, 0:META + w], AX))
                    sync()
                    dve.tensor_scalar(aneg[:, j:j + 1], amax[:, j:j + 1], -1.0, None, ALU.mult).then_inc(att_bias, 1)
                for j in range(QT):
                    w = META + (j + 1) * P
                    dve.wait_ge(att_exp, i * QT + (j + 1))
                    step(dve.reciprocal(ainv[:, j:j + 1], asum[:, j:j + 1]))
                    sync()
                    dve.tensor_scalar(ap_[:, j, 0:w], ap_[:, j, 0:w], ainv[:, j:j + 1], None, ALU.mult)\
                        .then_inc(att_probs, 1)
                for _ in range(QT + 2):
                    at.take()
            drained(gm)
            with repeat(dve, 2, [(gm, 4)]) as i:
                for c in range(4):
                    bn = gm.take()
                    b = full(bn)
                    dve.tensor_tensor(at_y[:, c % 2, :], psum[:, b, :], row(sga, i * 4 + c, 0, S), ALU.mult)\
                        .then_inc(bank_free[b], 1)
                    dve.wait_ge(bank_free[b], bn[1] + 2)
                    m = row(merged, i * 4 + c, 0, S)
                    dve.tensor_tensor(m, m, at_y[:, c % 2, :], ALU.add).then_inc(merged_done, 1)
            add_to_stream(2)
            drained(gm)
            swiglu("ffn2", FULL, META)
            norm(xT, nT, "final2", off=META)
            totals.append((gm.value(), at.value()))

        @block.gpsimd
        def _(pool):
            for j in range(SLOTS):
                pool.sem_inc(u_used[j], 1)
                pool.sem_inc(v_used[j], 1)
            turns = PICKS // TURN
            for tt in range(QT):
                pool.wait_ge(picked, tt + 1)
                picks = eidx[:, tt, :].rearrange("p (g j) -> p g j", j=GROUP)
                with pool.Fori(tt * turns, (tt + 1) * turns) as i:
                    for g in range(4):
                        pool.tensor_copy(pick[:, g, :], picks[:, bass.ds(i * 4 + (g - tt * turns * 4), 1), :]
                                         .rearrange("p a j -> p (a j)")).then_inc(pick_copied, 1)
                        pool.wait_ge(pick_copied, i * 4 + (g + 1))
                        for j in range(GROUP):
                            slot = g % 2 * GROUP + j
                            index = bass.IndirectOffsetOnAxis(pick[:, g, j:j + 1], 0)
                            pool.wait_ge(u_used[slot], i * 2 + (g // 2 + 1))
                            pool.sem_inc(pool_passed, 1)
                            pool.indirect_dma_start(u_rows[:, slot, :], None, peer_u_d, index)\
                                .then_inc(u_landed[slot], 16)
                            pool.wait_ge(v_used[slot], i * 2 + (g // 2 + 1))
                            pool.sem_inc(pool_passed, 1)
                            pool.indirect_dma_start(v_rows[:, slot, :], None, peer_v_d, index)\
                                .then_inc(v_landed[slot], 16)

        assert totals[0][0] == n_slabs and totals[0][1:] == totals[1] == totals[2], totals


def lay_slabs(ins):
    out = []

    def cols(w, m, k0=0, nk=KT):
        block = np.zeros((P, KT, P), np.float32)
        block[:, 0:nk] = w[k0 * P:(k0 + nk) * P, m * P:(m + 1) * P].reshape(nk, P, P).transpose(1, 0, 2)
        out.append(block.reshape(P, D))

    w = ins["w_in"][0]
    sc_b, sc_c, sc_x, cf_a, cf_g, g_sc, g_cf = (w[:, n * D:(n + 1) * D] for n in range(7))
    for m in range(KT):
        for part in (cf_a, cf_g, sc_c, sc_x, sc_b):
            cols(part, m)
    for m in range(KT):
        for part in (g_sc, ins["sc_w_out"][0], g_cf, ins["cf_w_pw2"][0]):
            cols(part, m)
    for m in range(KT):
        cols(ins["w_mix_out"][0], m)
    kv, q = ins["w_kv"][0], ins["w_q"][0]
    for h in range(XA_HEADS):
        for part in (kv[:, 0:D], kv[:, D:2 * D], q):
            cols(part, 2 * h)
            cols(part, 2 * h + 1)
    for m in range(KT):
        cols(ins["w_xo"][0], m)
    for m in range(2 * PEER_HEADS):
        cols(ins["w_peer_q"][0], m)

    def swiglu(n):
        for f in range(FT):
            cols(ins[f"ffn{n}_w_up_2"][0], f)
            cols(ins[f"ffn{n}_w_gate_2"][0], f)
        for m in range(KT):
            for k0, nk in ((0, 8), (8, 8), (16, 6)):
                cols(ins[f"ffn{n}_w_down_2"][0], m, k0, nk)

    swiglu(1)
    w, parts, a = ins["w_in_2"][0], [], 0
    for n in (D, D, 2 * D, 2 * D, D, D, D, 512, 64, 8, D, D):
        parts.append(w[:, a:a + n])
        a += n
    rq, rk, rv, rg, aq, ak, av, iq, ik, iw, g_ret, g_att = parts
    for m in range(4):
        cols(iq, m)
    cols(np.concatenate([ik, ik], 1), 0)
    for h in range(RET_HEADS):
        for part, n in ((rq, 2), (rk, 2), (rv, 4), (rg, 4)):
            for m in range(n):
                cols(part, n * h + m)
    for m in range(KT):
        cols(g_ret, m)
        cols(ins["w_ret_out_2"][0], m, 0)
        cols(ins["w_ret_out_2"][0], m, 8)
    for h in range(ATT_HEADS):
        for part in (aq, ak, av, g_att):
            cols(part, h)
    for name in ("w_att_out_2", "w_mix_out_2"):
        for m in range(KT):
            cols(ins[name][0], m)
    swiglu(2)
    return np.stack(out), np.ascontiguousarray(iw.reshape(KT, P, IDX_HEADS).transpose(1, 0, 2))


def tiles(x):
    return np.ascontiguousarray(x.T.reshape(-1, P, x.shape[0]).transpose(1, 0, 2))


def lay_vectors(ins):
    v = np.zeros((P, NVEC), np.float32)
    b1 = ins["cf_b_pw1"][0]
    for name, x in (("norm_mix", ins["norm_mix_g"]), ("b1a", b1[:D]), ("b1g", b1[D:]), ("cf_b", ins["cf_conv_b"]),
                    ("ln_g", ins["cf_ln_g"]), ("ln_b", ins["cf_ln_b"]), ("pw2_b", ins["cf_b_pw2"]),
                    ("norm_xa", ins["norm_xa_g"]), ("norm_mem", ins["norm_mem_g"]),
                    ("norm_peer", ins["norm_peer_g"]), ("final1", ins["final_norm_g"]),
                    ("ffn1", ins["ffn1_norm_2"]), ("mix2", ins["mix_norm_2"]), ("ffn2", ins["ffn2_norm_2"]),
                    ("final2", ins["final_norm_2"])):
        v[:, VECS[name]:VECS[name] + KT] = x.reshape(KT, P).T
    for name, x, taps in (("sc_w", ins["sc_conv_w"][0], SC_K), ("cf_w", ins["cf_conv_w"][0], CF_K)):
        v[:, VECS[name]:VECS[name] + KT * taps] = x.reshape(taps, KT, P).transpose(2, 1, 0).reshape(P, KT * taps)
    return v


def constants():
    c = np.zeros((P, NCONST), np.float32)
    c[:, 0:P] = np.eye(P)
    c[:, P:2 * P] = 1.0
    c[:, 2 * P:3 * P] = np.tril(np.ones((P, P)))
    c[:, 3 * P:FIXED] = np.arange(TOPK)
    pos = np.arange(T2, dtype=np.float32)
    at = TABLES
    for dim in (256, 128, 64):
        freq = (np.float32(THETA) ** (-np.arange(0, dim, 2, dtype=np.float32) / np.float32(dim))).astype(np.float32)
        angle = (freq[:, None] * pos[None, :]).astype(np.float32)
        half = dim // 2
        reps = P // half
        sign = np.ones(P) if dim == 256 else np.where((np.arange(P) // half) % 2 == 0, 1.0, -1.0)
        c[:, at:at + T2] = np.tile(np.cos(angle), (reps, 1))
        c[:, at + T2:at + 2 * T2] = np.tile(np.sin(angle), (reps, 1)) * sign[:, None]
        at += 2 * T2
    log_g = np.log1p(-(2.0 ** (-5.0 - np.arange(RET_HEADS))))
    key, query = np.arange(P)[:, None], np.arange(S)[None, :]
    meta = np.zeros((META, RET_HEADS * S), np.float32)
    for h in range(RET_HEADS):
        d = query - key
        c[:, DECAY + h * S:DECAY + (h + 1) * S] = np.where(d >= 0, np.exp(log_g[h] * np.maximum(d, 0)), 0) * RET_DK ** -0.5
        meta[:, h * S:(h + 1) * S] = np.exp(log_g[h] * (query + META - key[:META])) * RET_DK ** -0.5
    return c, meta


def kernel(**inputs):
    import concourse.bacc as bacc
    from concourse.bass_utils import run_bass_kernel_spmd

    ins = {k: np.asarray(v) for k, v in inputs.items()}
    slabs, wi = lay_slabs(ins)
    consts, consts16 = constants()
    arrays = {
        "slabs": slabs,
        "xT": tiles(ins["x"][0]),
        "memT": tiles(ins["mem"][0]),
        "metaT": tiles(ins["meta_tokens_2"]),
        "vecs": lay_vectors(ins),
        "consts": consts,
        "consts16": consts16,
        "subkeys": np.ascontiguousarray(ins["peer_subkeys"][0].transpose(2, 0, 1)),
        "wi": wi,
        "peer_u": np.ascontiguousarray(ins["peer_u"][0]),
        "peer_v": np.ascontiguousarray(ins["peer_v"][0]),
    }
    nc = bacc.Bacc("TRN2", target_bir_lowering=False, num_devices=1)
    args = [nc.dram_tensor("in_" + name, a.shape, F32, kind="ExternalInput").ap() for name, a in arrays.items()]
    out = nc.dram_tensor("outT", (P, KT, S), F32, kind="ExternalOutput").ap()
    build(nc, *args, out, slabs.shape[0])
    got = run_bass_kernel_spmd(nc, [{"in_" + n: a for n, a in arrays.items()}], core_ids=[0]).results[0]["outT"]
    return np.ascontiguousarray(got.reshape(P, KT, S).transpose(2, 1, 0).reshape(1, S, D))
```

```python
from contextlib import ExitStack, contextmanager

import numpy as np

import concourse.bass as bass
from concourse import mybir

F32 = mybir.dt.float32
F32R = mybir.dt.float32r
BF16 = mybir.dt.bfloat16
U32 = mybir.dt.uint32
ACT = mybir.ActivationFunctionType
ALU = mybir.AluOpType
AX = mybir.AxisListType.X

P = 128
D = 1024
KT = D // P
S = 512
QT = S // P
META = 16
T2 = S + META
HALF = T2 // 2
EPS = 1e-6
MEM = 256
MT = MEM // P
SC_K, CF_K = 3, 31
XA_HEADS, XA_DT = 4, 2
XA_SCALE = 256 ** -0.5
PEER_HEADS, TOPK = 8, 16
PICKS = PEER_HEADS * TOPK
EXPERTS = 128 * 128
FF = 2816
FT = FF // P
RET_HEADS, RET_DK, RET_DV = 4, 256, 512
ATT_HEADS = 8
ATT_SCALE = 128 ** -0.5
IDX_HEADS, IDX_DH = 8, 64
IDX_SCALE = (IDX_DH ** -0.5) * (IDX_HEADS ** -0.5)
KEEP = 128
THETA = 10000.0
RAW = 2
READY = 4
SLOTS = 8
GROUP = 4
TURN = 4 * GROUP
FAR = -3.0e38
TAKEN = -3.2e38
FLOOR = -3.4e38
HIDE = -1.0e30

VECS = {}
_at = 0
for _name, _n in (("norm_mix", 8), ("b1a", 8), ("b1g", 8), ("sc_w", 8 * SC_K), ("cf_w", 8 * CF_K), ("cf_b", 8),
                  ("ln_g", 8), ("ln_b", 8), ("pw2_b", 8), ("norm_xa", 8), ("norm_mem", 8), ("norm_peer", 8),
                  ("final1", 8), ("ffn1", 8), ("mix2", 8), ("ffn2", 8), ("final2", 8)):
    VECS[_name] = _at
    _at += _n
NVEC = _at

FIXED = 3 * P + TOPK
TABLES = FIXED
DECAY = TABLES + 6 * T2
NCONST = DECAY + (RET_HEADS + 1) * S
NORMS = 10


class Counter:

    def __init__(self):
        self.base, self.k, self.i, self.per = 0, 0, None, 0

    def enter(self, i, per):
        assert self.i is None
        self.base, self.k = self.base + self.k, 0
        self.i, self.per = i, per

    def leave(self, n):
        assert self.k == self.per, f"a turn of the loop counts {self.k}, not {self.per}"
        self.base, self.k, self.i = self.base + n * self.per, 0, None

    def value(self, shift=0):
        now = self.base + self.k + shift
        return now if self.i is None else self.i * self.per + now


class Ring(Counter):

    def __init__(self, n, first=0):
        super().__init__()
        self.n, self.first = n, first

    def take(self):
        now = self.base + self.k
        self.k += 1
        slot, before = now % self.n, now // self.n
        if self.i is not None:
            assert self.per % self.n == 0
            before = self.i * (self.per // self.n) + before
        return self.first + slot, before

    def taken(self):
        now = self.base + self.k
        return [(self.first + s, (now + self.n - 1 - s) // self.n) for s in range(self.n)]


class Chain(Counter):

    def __init__(self, eng, sem):
        super().__init__()
        self.eng, self.sem = eng, sem

    def step(self, ins):
        ins.then_inc(self.sem, 1)
        self.k += 1

    def wait(self, back=0):
        self.eng.wait_ge(self.sem, self.value(-back))


@contextmanager
def repeat(eng, n, counters):
    with eng.Fori(0, n) as i:
        for c, per in counters:
            c.enter(i, per)
        yield i
    for c, _ in counters:
        c.leave(n)


def row(t, index, a, b):
    return t[:, bass.ds(index, 1), a:b].rearrange("p a n -> p (a n)")


def build(nc, slabs_d, xT_d, memT_d, metaT_d, vecs_d, consts_d, consts16_d, subk_d, wi_d, peer_u_d, peer_v_d, out_d,
          n_slabs):
    ctx = ExitStack()
    with ctx:
        def sb(name, shape, dt=F32):
            return ctx.enter_context(nc.sbuf_tensor(name, shape, dt))

        def sem(name):
            return ctx.enter_context(nc.semaphore(name))

        raw = sb("raw_slabs", [P, RAW, D])
        slab_h = sb("slabs_rounded", [P, READY, D], F32R)
        slab_l = sb("slabs_remainder", [P, READY, D], F32R)
        xT = sb("xT", [P, KT, T2])
        vecs = sb("vecs", [P, NVEC])
        fixed = sb("fixed", [P, FIXED])
        ident, ones = fixed[:, 0:P], fixed[:, P:2 * P]
        tri = fixed[:, 2 * P:3 * P]
        iota16 = fixed[:, 3 * P:FIXED]
        zeros = sb("zeros", [P, S], BF16)
        zero = sb("zero", [P, 1])
        norm_ms = sb("norm_mean_square", [P, T2])
        norm_rs = sb("norm_recip_root", [P, T2])

        OPERAND = KT * T2
        ARENA = 28160 + 2 * OPERAND
        arena_at = nc.sbuf_base
        sb("arena", [P, ARENA])
        n_placed = [0]

        class Part:

            def __init__(self, at=0):
                self.at = at

            def __call__(self, *shape, dt=F32, rows=P):
                n_placed[0] += 1
                v = nc.alloc_sbuf_tensor_at(f"buffer_{n_placed[0]}_{dt.name}", [rows, *shape], dt,
                                            offset=arena_at + 4 * self.at).ap()
                n = int(np.prod(shape)) // (2 if dt is BF16 else 1)
                self.at += -(-n // 8) * 8
                assert self.at <= ARENA, self.at
                return v

        part = Part()
        op = (part(KT, T2, dt=F32R), part(KT, T2, dt=F32R))
        base = part.at
        SQ = ARENA - KT * T2
        sq = Part(SQ)(KT, T2)
        part = Part(base)
        merged = part(KT, S)
        shared = part.at
        scy = (part(KT, S, dt=F32R), part(KT, S, dt=F32R))
        cfc_at = part.at
        cfc = part(KT, S)
        cfp = part(2, CF_K - 1 + S)
        scp = part(2, SC_K - 1 + S)
        sg = part(2, S)
        xs = part(2, S)
        sct = part(2, S)
        acc_e = part(S)
        acc_o = part(S)
        mu = part(S)
        assert part.at <= SQ
        cfs = (Part(SQ)(KT, S, dt=F32R), Part(cfc_at)(KT, S, dt=F32R))
        part = Part(shared)
        memT = part(KT, MEM)
        memN = (part(KT, MEM, dt=F32R), part(KT, MEM, dt=F32R))
        oT = part(KT, S)
        xk = part(2, XA_DT * MEM)
        xv = part(2, MT * 256)
        xq = part(2, XA_DT * S)
        xp = part(2, QT * MEM)
        xpt = part(2, MT * S)
        xmax = part(2, QT)
        xneg = part(2, QT)
        xsum = part(2, QT)
        xinv = part(2, QT)
        assert part.at <= SQ
        B2 = 2 * PEER_HEADS
        part = Part(base)
        sub_s = part(QT, B2, P)
        hrow = part(QT, D)
        eidx = part(QT, PICKS, dt=U32)
        gates = part(QT, PICKS)
        tk_wk = part(B2, P)
        cand_wk = tk_wk.rearrange("p (h a) n -> p h (a n)", h=PEER_HEADS)
        tk_v = part(B2, TOPK)
        tk_i = part(B2, TOPK, dt=U32)
        tk_f = part(B2, TOPK)
        fin_v = part(PEER_HEADS, TOPK)
        fin_e = part(PEER_HEADS, TOPK)
        fin_p = part(PEER_HEADS, TOPK, dt=U32)
        fin_a = part(PEER_HEADS, TOPK, dt=U32)
        fin_b = part(PEER_HEADS, TOPK, dt=U32)
        fin_af = part(PEER_HEADS, TOPK)
        fin_bf = part(PEER_HEADS, TOPK)
        fin_i0 = part(PEER_HEADS, TOPK)
        fin_i1 = part(PEER_HEADS, TOPK)
        fin_s = part(PEER_HEADS)
        fin_r = part(PEER_HEADS)
        subk = Part(part.at)(2, P)
        diag = part(SLOTS, P)
        dots = part(4, GROUP)
        acts = part(4, GROUP)
        coefs = part(4, GROUP)
        pick = part(4, GROUP, dt=U32)
        dump = part(D, dt=BF16)
        out_rows = part(D)
        assert part.at <= ARENA - SLOTS * D, part.at
        pq = Part(ARENA - SLOTS * D)(4, S)
        v_rows = Part(ARENA - SLOTS * D)(SLOTS, D)
        u_rows = Part()(SLOTS, D)
        part = Part(base)
        silu = part(2, T2)
        hid_new = part(2, T2)
        sq_hid = Part()(KT, T2)
        hid = (part(FT, T2, dt=F32R), part(FT, T2, dt=F32R))
        part = Part(shared)
        key_bias = part(QT, S)
        work = key_bias[:, 1:QT, :]
        top8 = part(3, 8)
        yr_at = part.at
        yr = part(4 * RET_HEADS, S)
        mixer = part.at
        cos_i, sin_i = (part(T2) for _ in range(2))
        iq = part(4, S)
        ik = part(S)
        iw = part(QT, IDX_HEADS)
        wi = part(KT, IDX_HEADS)
        rope_t = part(2, T2)
        relu = part(2, S)
        score = part(3, S)
        assert part.at <= SQ
        part = Part(mixer)
        cos_r, sin_r = (part(T2) for _ in range(2))
        decay = part(S)
        decay_m = part(S, rows=META)
        rtm = part(4, META)
        rq = part(2, S)
        rk = part(2, S)
        rkm = part(2, META)
        rv = part(QT, S)
        rvm = part(S, rows=META)
        rg = part(4, S)
        rp = part(QT, S)
        rpm = part(S, rows=META)
        ry = part(4, S)
        rt = rp
        rsq = rp
        part = Part(mixer)
        yr_s = (part(4 * RET_HEADS, S, dt=F32R),
                Part(yr_at)(4 * RET_HEADS, S, dt=F32R))
        gs = part(KT, S)
        assert part.at <= ARENA - 2 * T2
        cos_a, sin_a = (Part(ARENA - n * T2)(T2) for n in (2, 1))
        part = Part(yr_at)
        oT2 = part(KT, S)
        av = part(QT, D)
        avm = part(D, rows=META)
        sga = part(KT, S)
        aq = part(S)
        ak = part(T2)
        at_t = part(2, S)
        at_tm = part(META)
        aptm = part(S, rows=META)
        amax = part(QT)
        aneg = part(QT)
        asum = part(QT)
        ainv = part(QT)
        apt = part(QT, S)
        ap_ = part(QT, T2)
        av_h = part(QT, P)
        avm_h = part(P, rows=META)
        at_y = ap_.rearrange("p a b -> p (a b)")[:, 0:2 * S].rearrange("p (a b) -> p a b", a=2)
        assert part.at <= ARENA - 2 * T2

        psum = ctx.enter_context(nc.psum_tensor("psum", [P, 8, 512], F32))

        slab_landed = [sem(f"slab_landed_{s}") for s in range(RAW)]
        slab_rounded = sem("slab_rounded")
        slab_ready = [sem(f"slab_ready_{s}") for s in range(READY)]
        rounded = sem("activation_rounded")
        split = sem("activation_split")
        slab_used = sem("slab_used")
        bank_full = [sem(f"bank_full_{b}") for b in range(8)]
        bank_free = [sem(f"bank_free_{b}") for b in range(8)]
        loaded = sem("constants_loaded")
        mem_loaded = sem("memory_loaded")
        subk_loaded = sem("subkeys_loaded")
        mixer_loaded = sem("mixer_constants_loaded")
        decay_loaded = sem("decay_loaded")
        cleared = sem("zero_cleared")
        dve_step = sem("dve_step")
        dve_passed = sem("dve_passed_a_wait")
        pool_passed = sem("pool_passed_a_wait")
        norm_sq = sem("norm_squares")
        tiles_summed = sem("channel_tiles_summed")
        norm_mean = sem("norm_mean_ready")
        norm_root = sem("norm_root")
        norm_out = sem("norm_done")
        cf_centred = sem("conformer_centred")
        cf_silu = sem("conformer_silu")
        merged_done = sem("merged_done")
        xa_bias = sem("xa_negative_max")
        xa_exp = sem("xa_exp")
        xa_probs = sem("xa_probs")
        gate_in = sem("peer_gate_shifted")
        gate_exp = sem("peer_gate_exp")
        picked = sem("peer_picked")
        pick_copied = sem("pick_copied")
        u_landed = [sem(f"u_landed_{j}") for j in range(SLOTS)]
        v_landed = [sem(f"v_landed_{j}") for j in range(SLOTS)]
        u_used = [sem(f"u_used_{j}") for j in range(SLOTS)]
        v_used = [sem(f"v_used_{j}") for j in range(SLOTS)]
        gelu_done = sem("gelu_done")
        coef_done = sem("coef_done")
        diag_done = [sem(f"diag_done_{j}") for j in range(SLOTS)]
        idx_rope = sem("index_rope_done")
        scy_made = sem("short_conv_made")
        relu_read = sem("relu_read")
        index_scored = sem("index_scores_done")
        ret_rope = sem("retention_rope_done")
        ret_sq = sem("retention_squares")
        ret_summed = sem("retention_squares_summed")
        ret_ms = sem("retention_mean_square")
        ret_root = sem("retention_root")
        ret_done = sem("retention_head_done")
        att_rope = sem("attention_rope_done")
        values_here = sem("attention_values_here")
        val_step = sem("attention_values_copied")
        att_bias = sem("attention_negative_max")
        att_exp = sem("attention_exp")
        att_probs = sem("attention_probs")
        stored = sem("stored")

        def vec(name, i):
            return vecs[:, VECS[name] + i:VECS[name] + i + 1]

        def vec_at(name, i, stride=1, shift=0):
            return vecs[:, bass.ds(i * stride + (VECS[name] + shift), 1)]

        def X(k):
            return xT[:, k, META:T2]

        FULL = ((0, S),)
        BLOCK2 = ((0, HALF), (HALF, HALF))

        totals, slabs_before_gathers = [], []
        block = ctx.enter_context(nc.Block())

        @block.sync
        def _(sp):
            for n in range(READY):
                if n >= RAW:
                    sp.wait_ge(slab_ready[n - RAW], 1)
                sp.dma_start(raw[:, n % RAW, :], slabs_d[n]).then_inc(slab_landed[n % RAW], 16)
            turns = n_slabs // READY
            with sp.Fori(1, turns) as i:
                for j in range(READY):
                    if j < RAW:
                        sp.wait_ge(slab_ready[j + READY - RAW], i)
                    else:
                        sp.wait_ge(slab_ready[j - RAW], i + 1)
                    sp.dma_start(raw[:, j % RAW, :],
                                 slabs_d[bass.ds(i * READY + j, 1)].rearrange("o p n -> (o p) n"))\
                        .then_inc(slab_landed[j % RAW], 16)
            for n in range(turns * READY, n_slabs):
                before = n - RAW
                sp.wait_ge(slab_ready[before % READY], before // READY + 1)
                sp.dma_start(raw[:, n % RAW, :], slabs_d[n]).then_inc(slab_landed[n % RAW], 16)
            sp.wait_ge(norm_out, KT * NORMS)
            sp.dma_start(out_d, sq[:, :, 0:S]).then_inc(stored, 16)
            sp.wait_ge(stored, 16)

        @block.tensor
        def _(pe):
            slabs, gm, at = Ring(READY), Ring(4), Ring(4, 4)
            splits, sums = [0], [0]

            def claim(ring):
                b, n = ring.take()
                pe.wait_ge(bank_free[b], n + 1)
                return b

            def drained(ring):
                for b, n in ring.taken():
                    if n:
                        pe.wait_ge(bank_free[b], n + 1)

            class Slab:

                def __init__(self):
                    self.slot, n = slabs.take()
                    pe.wait_ge(slab_ready[self.slot], n + 1)
                    self.told = False

                def add(self, out, tile, x, start, stop, values=False, width=P):
                    wh, wl = (w[:, self.slot, tile * width:(tile + 1) * width] for w in (slab_h, slab_l))
                    xh, xl = x
                    for j, (w, y) in enumerate(((wh, xh), (wh, xl), (wl, xh))):
                        a, b = (y, w) if values else (w, y)
                        m = pe.matmul(out, a, b, start=start and j == 0, stop=stop and j == 2)
                        if not self.told:
                            m.then_inc(slab_used, 1)
                            self.told = True
                    return m

            def cols(x, k, a, b):
                return tuple(t[:, k, a:b] for t in x)

            def await_split(n=KT):
                splits[0] += n
                pe.wait_ge(split, splits[0])

            def coming(n=KT):
                splits[0] += n
                return splits[0] - n

            def product(rhs, parts=FULL, off=0, since=None):
                w = Slab()
                for a, n in parts:
                    b = claim(gm)
                    for k in range(KT):
                        if since is not None and a == 0:
                            pe.wait_ge(split, since + k + 1)
                        m = w.add(psum[:, b, 0:n], k, cols(rhs, k, off + a, off + a + n), k == 0, k == KT - 1)
                    m.then_inc(bank_full[b], 1)

            def product_k(rhs, meta, col):
                w = Slab()
                for k in range(KT):
                    m = w.add(psum[:, meta, col:col + META], k, cols(rhs, k, 0, META), k == 0, k == KT - 1)
                b = claim(gm)
                for k in range(KT):
                    m2 = w.add(psum[:, b, :], k, cols(rhs, k, META, T2), k == 0, k == KT - 1)
                m2.then_inc(bank_full[b], 1)
                return m

            def product_rows(lhs, tiles, width, off=0, meta=None):
                banks = [claim(gm) for _ in range(tiles)]
                at_once = D // width
                for s in range(KT // at_once):
                    w = Slab()
                    for j in range(at_once):
                        k = s * at_once + j
                        how = (k == 0, k == KT - 1, True, width)
                        if meta is not None:
                            m = w.add(psum[:, meta, 0:width], j, cols(lhs, k, 0, P), *how)
                            if k == KT - 1:
                                m.then_inc(bank_full[meta], 1)
                        for tt, b in enumerate(banks):
                            m = w.add(psum[:, b, 0:width], j, cols(lhs, k, off + tt * P, off + (tt + 1) * P), *how)
                            if k == KT - 1:
                                m.then_inc(bank_full[b], 1)

            def column_sums(parts=FULL):
                sums[0] += 1
                pe.wait_ge(tiles_summed, sums[0])
                for a, n in parts:
                    b = claim(at)
                    pe.matmul(psum[:, b, 0:n], ones[:, :], norm_rs[:, a:a + n], start=True, stop=True)\
                        .then_inc(bank_full[b], 1)

            def norm(parts=FULL):
                column_sums(parts)
                return coming()

            for b in range(8):
                pe.sem_inc(bank_free[b], 1)
            pe.wait_ge(loaded, 16 * 6)
            since = norm()
            with repeat(pe, 2, [(slabs, 20), (gm, 20)]):
                for c in range(4):
                    for j in range(5):
                        product(op, since=None if c or j else since)
            with repeat(pe, 2, [(slabs, 4), (gm, 4)]):
                for _ in range(4):
                    product(op)
            column_sums()
            await_split()
            with repeat(pe, 2, [(slabs, 4), (gm, 4)]):
                for _ in range(4):
                    product(scy)
            column_sums()
            since = coming()
            with repeat(pe, 4, [(slabs, 4), (gm, 4)]):
                for c in range(2):
                    product(op)
                    product(cfs, since=None if c else since)
            since = coming()
            for m in range(KT):
                product(op, since=None if m else since)
                if m == 3:
                    norm(((0, MEM),))

            since = norm()

            def peek(ring, back):
                now = ring.base + ring.k - back
                n = now // ring.n + 1
                if ring.i is not None:
                    n = ring.i * (ring.per // ring.n) + n
                return ring.first + now % ring.n, n

            with repeat(pe, 2, [(slabs, 12), (gm, 12), (at, 20)]) as i:
                for h in range(2):
                    for d in range(XA_DT):
                        product(memN, ((0, MEM),), since=None if h or d else since - KT)
                    product_rows(memN, MT, XA_DT * P)
                    for d in range(XA_DT):
                        product(op, since=None if h or d else since)
                    for back in range(6, 0, -1):
                        b, n = peek(gm, back)
                        pe.wait_ge(bank_free[b], n + 1)
                    for j in range(QT):
                        b = claim(at)
                        for d in range(XA_DT):
                            m = pe.matmul(psum[:, b, 0:MEM], xq[:, h, d * S + j * P:d * S + (j + 1) * P],
                                          xk[:, h, d * MEM:(d + 1) * MEM], start=d == 0, stop=d == XA_DT - 1)
                        m.then_inc(bank_full[b], 1)
                    for j in range(QT):
                        pe.wait_ge(xa_probs, i * (2 * QT) + (h * QT + j + 1))
                        b = claim(at)
                        for t in range(MT):
                            m = pe.transpose(psum[:, b, t * P:(t + 1) * P],
                                             xp[:, h, j * MEM + t * P:j * MEM + (t + 1) * P], ident[:, :])
                        m.then_inc(bank_full[b], 1)
                    for back in range(4, 0, -1):
                        b, n = peek(at, back)
                        pe.wait_ge(bank_free[b], n + 1)
                    for e in range(XA_DT):
                        b = claim(at)
                        for t in range(MT):
                            m = pe.matmul(psum[:, b, :], xv[:, h, t * 256 + e * P:t * 256 + (e + 1) * P],
                                          xpt[:, h, t * S:(t + 1) * S], start=t == 0, stop=t == MT - 1)
                        m.then_inc(bank_full[b], 1)
            since = coming()
            with repeat(pe, 2, [(slabs, 4), (gm, 4)]):
                for c in range(4):
                    product(op, since=None if c else since)

            since = norm()
            pe.wait_ge(subk_loaded, 16)

            def subscores(j):
                b, n = peek(gm, 1)
                pe.wait_ge(bank_free[b], n + 1)
                b = claim(at)
                for tt in range(QT):
                    m = pe.matmul(psum[:, b, tt * P:(tt + 1) * P], pq[:, j, tt * P:(tt + 1) * P],
                                  subk[:, j % 2, :], start=True, stop=True)
                m.then_inc(bank_full[b], 1)

            with repeat(pe, 4, [(slabs, 4), (gm, 4), (at, 4)]):
                for j in range(4):
                    product(op, since=None if j else since)
                    subscores(j)
            slabs_before_gathers.append(slabs.value())
            for tt in range(QT):
                for q in range(2):
                    b = claim(at)
                    for k in range(4):
                        m = pe.transpose(psum[:, b, k * P:(k + 1) * P], sq[:, 4 * q + k, tt * P:(tt + 1) * P],
                                         ident[:, :])
                    m.then_inc(bank_full[b], 1)
            for tt in range(QT):
                banks, frees = [], []
                for q in range(2):
                    banks.append(claim(at))
                    frees.append(peek(at, 1))
                for q in range(2):
                    pe.matmul(psum[:, banks[q], :], zeros[:, 0:P], zeros[:, :], start=True, stop=False)
                with pe.Fori(tt * (PICKS // SLOTS), (tt + 1) * (PICKS // SLOTS)) as i:
                    for j in range(SLOTS):
                        pe.wait_ge(diag_done[j], i + 1)
                        pe.wait_ge(v_landed[j], i * 16 + 16)
                        for q in range(2):
                            m = pe.matmul(psum[:, banks[q], :], diag[:, j, :], v_rows[:, j, q * 512:(q + 1) * 512],
                                          start=False, stop=False)
                        m.then_inc(v_used[j], 1)
                for q in range(2):
                    pe.matmul(psum[:, banks[q], :], zeros[:, 0:P], zeros[:, :], start=False, stop=True)\
                        .then_inc(bank_full[banks[q]], 1)
                for q in range(2):
                    pe.wait_ge(bank_free[frees[q][0]], frees[q][1] + 1)
                    b = claim(at)
                    for k in range(4):
                        m = pe.transpose(psum[:, b, k * P:(k + 1) * P],
                                         out_rows[:, (4 * q + k) * P:(4 * q + k + 1) * P], ident[:, :])
                    m.then_inc(bank_full[b], 1)
            column_sums()

            def swiglu(parts, off):
                since = norm(parts)
                with repeat(pe, FT // 2, [(slabs, 4), (gm, 4 * len(parts))]):
                    for c in range(2):
                        product(op, parts, since=None if c else since)
                        product(op, parts)
                await_split(FT)
                with repeat(pe, 2, [(slabs, 12), (gm, 4 * len(parts))]):
                    for _ in range(4):
                        banks = [claim(gm) for _ in parts]
                        for s, nk in enumerate((8, 8, 6)):
                            w = Slab()
                            for b, (a, n) in zip(banks, parts):
                                for k in range(nk):
                                    f = 8 * s + k
                                    m = w.add(psum[:, b, 0:n], k, cols(hid, f, a, a + n), f == 0, f == FT - 1)
                                if s == 2:
                                    m.then_inc(bank_full[b], 1)

            swiglu(BLOCK2, 0)

            since = norm(BLOCK2)
            for c in range(4):
                product(op, FULL, META, None if c else since)
            product(op, FULL, META)
            pe.wait_ge(mixer_loaded, 16 * 3)
            b = claim(at)
            for tt in range(QT):
                for k in range(KT):
                    m = pe.matmul(psum[:, b, tt * 8:tt * 8 + 8], sq[:, k, META + tt * P:META + (tt + 1) * P],
                                  wi[:, k, :], start=k == 0, stop=k == KT - 1)
            m.then_inc(bank_full[b], 1)
            pe.wait_ge(idx_rope, 5)
            for j in range(1, QT):
                for h in range(IDX_HEADS):
                    b = claim(at)
                    r = 64 * (h % 2)
                    pe.matmul(psum[:, b, 0:(j + 1) * P], iq[r:r + 64, h // 2, j * P:(j + 1) * P],
                              ik[r:r + 64, 0:(j + 1) * P], start=True, stop=True).then_inc(bank_full[b], 1)
            drained(gm)

            with repeat(pe, RET_HEADS, [(slabs, 12), (gm, 12), (at, 12)]) as i:
                for _ in range(2):
                    product(op, FULL, META)
                km = claim(at)
                for d in range(2):
                    m = product_k(op, km, d * META)
                m.then_inc(bank_full[km], 1)
                product_rows(op, QT, RET_DV, META, claim(at))
                for _ in range(4):
                    product(op, FULL, META)
                pe.wait_ge(ret_rope, i * 3 + 3)
                b = claim(at)
                for d in range(2):
                    m = pe.matmul(psum[0:META, b, :], rkm[:, d, :], rq[:, d, :], start=d == 0, stop=d == 1)
                m.then_inc(bank_full[b], 1)
                for s in range(QT):
                    b = claim(at)
                    for d in range(2):
                        m = pe.matmul(psum[:, b, 0:S - s * P], rk[:, d, s * P:(s + 1) * P], rq[:, d, s * P:S],
                                      start=d == 0, stop=d == 1)
                    m.then_inc(bank_full[b], 1)
                for back in range(8, 4, -1):
                    b, n = peek(gm, back)
                    pe.wait_ge(bank_free[b], n + 1)
                b, n = peek(at, 6)
                pe.wait_ge(bank_free[b], n + 1)
                for back in range(5, 0, -1):
                    b, n = peek(at, back)
                    pe.wait_ge(bank_free[b], n + 1)
                for e in range(4):
                    b = claim(at)
                    pe.matmul(psum[:, b, :], rvm[:, e * P:(e + 1) * P], rpm[:, :], start=True, stop=False)
                    for s in range(QT):
                        m = pe.matmul(psum[:, b, s * P:S], rv[:, s, e * P:(e + 1) * P], rp[:, s, s * P:S],
                                      start=False, stop=s == QT - 1)
                    m.then_inc(bank_full[b], 1)
                b = claim(at)
                pe.wait_ge(ret_summed, i + 1)
                pe.matmul(psum[:, b, :], ones[:, :], rsq[:, 0, :], start=True, stop=True).then_inc(bank_full[b], 1)
            pe.wait_ge(ret_done, 4 * RET_HEADS)
            with repeat(pe, 2, [(slabs, 4), (gm, 4)]):
                for _ in range(4):
                    product(op, FULL, META)
            await_split(4 * RET_HEADS)
            with repeat(pe, 2, [(slabs, 8), (gm, 4)]):
                for _ in range(4):
                    b = claim(gm)
                    for s in range(2):
                        w = Slab()
                        for k in range(KT):
                            m = w.add(psum[:, b, :], k, cols(yr_s, 8 * s + k, 0, S), s + k == 0,
                                      s == 1 and k == KT - 1)
                    m.then_inc(bank_full[b], 1)
            for _ in range(2):
                product_rows(op, QT, S, META, claim(at))
            with repeat(pe, ATT_HEADS // 4, [(slabs, 12), (gm, 12), (at, 48)]) as i:
                for h in range(4):
                    product(op, FULL, META)
                    kv = claim(at)
                    product_k(op, kv, 0).then_inc(bank_full[kv], 1)
                    product(op, FULL, META)
                    pe.wait_ge(att_rope, i * 12 + (3 * h + 3))
                    b = claim(at)
                    for j in range(QT):
                        m = pe.matmul(psum[:, b, j * META:(j + 1) * META], aq[:, j * P:(j + 1) * P], ak[:, 0:META],
                                      start=True, stop=True)
                    m.then_inc(bank_full[b], 1)
                    for j in range(QT):
                        b = claim(at)
                        pe.matmul(psum[:, b, 0:(j + 1) * P], aq[:, j * P:(j + 1) * P], ak[:, META:META + (j + 1) * P],
                                  start=True, stop=True).then_inc(bank_full[b], 1)
                    for j in range(QT):
                        pe.wait_ge(att_probs, i * (4 * QT) + (h * QT + j + 1))
                        b = claim(at)
                        for s in range(j + 1):
                            m = pe.transpose(psum[:, b, s * P:(s + 1) * P], ap_[:, j, META + s * P:META + (s + 1) * P],
                                             ident[:, :])
                        m.then_inc(bank_full[b], 1)
                    b = claim(at)
                    for j in range(QT):
                        m = pe.transpose(psum[0:META, b, j * P:(j + 1) * P], ap_[:, j, 0:META], ident[:, :])
                    m.then_inc(bank_full[b], 1)
                    for back in (5, 4, 3, 2, 1):
                        b, n = peek(at, back)
                        pe.wait_ge(bank_free[b], n + 1)
                    pe.wait_ge(values_here, i * 4 + (h + 1))
                    b = claim(at)
                    pe.matmul(psum[:, b, :], avm_h, aptm[:, :], start=True, stop=False)
                    for s in range(QT):
                        m = pe.matmul(psum[:, b, s * P:S], av_h[:, s, :], apt[:, s, s * P:S], start=False, stop=s == QT - 1)
                    m.then_inc(bank_full[b], 1)
            since = coming()
            with repeat(pe, 2, [(slabs, 4), (gm, 4)]):
                for c in range(4):
                    product(op, since=None if c else since)
            since = coming()
            with repeat(pe, 2, [(slabs, 4), (gm, 4)]):
                for c in range(4):
                    product(op, since=None if c else since)
            swiglu(FULL, META)
            column_sums()
            totals.append((slabs.value(), gm.value(), at.value()))

        @block.scalar
        def _(act):
            gm, at = Ring(4), Ring(4, 4)
            norms, splits = [0], [0]

            def full(bn):
                act.wait_ge(bank_full[bn[0]], bn[1] + 1)
                return bn[0]

            def drained(ring):
                for b, n in ring.taken():
                    if n:
                        act.wait_ge(bank_free[b], n + 1)

            def round_(dst, src):
                act.activation(dst, src, ACT.Copy).then_inc(rounded, 1)

            def norm(src, parts=FULL, off=0, dst=op, made=None, after_norm=False, squares=sq):
                T = parts[-1][0] + parts[-1][1]
                for k in range(KT):
                    for b, n in made[k] if made else ():
                        act.wait_ge(bank_free[b], n + 2)
                    if after_norm:
                        act.wait_ge(norm_out, KT * (norms[0] - 1) + k + 1)
                    act.activation(squares[:, k, 0:T], src[:, k, off:off + T], ACT.Square).then_inc(norm_sq, 1)
                for _ in parts:
                    at.take()
                act.wait_ge(norm_mean, norms[0] + 1)
                act.activation(norm_rs[:, 0:T], norm_ms[:, 0:T], ACT.Sqrt).then_inc(norm_root, 1)
                norms[0] += 1
                if dst:
                    for k in range(KT):
                        act.wait_ge(norm_out, KT * (norms[0] - 1) + k + 1)
                        round_(dst[0][:, k, 0:T], sq[:, k, 0:T])
                    splits[0] += KT
                    act.wait_ge(split, splits[0])

            for k in range(0, KT, 2):
                act.dma_start(xT[:, k:k + 2, META:T2], xT_d[:, k:k + 2, :]).then_inc(loaded, 16)
            act.dma_start(vecs[:, :], vecs_d).then_inc(loaded, 16)
            act.dma_start(fixed[:, :], consts_d[:, 0:FIXED]).then_inc(loaded, 16)
            act.dma_start(xT[:, :, 0:META], metaT_d).then_inc(mem_loaded, 16)
            act.wait_ge(loaded, 16 * 6)
            norm(xT, off=META)

            with repeat(act, 2, [(gm, 20)]) as i:
                for c in range(4):
                    a, g, sc, sx, sb_ = (gm.take() for _ in range(5))
                    b = full(g)
                    act.activation(sg[:, c % 2, :], psum[:, b, :], ACT.Sigmoid, bias=vec_at("b1g", i, 4, c))\
                        .then_inc(bank_free[b], 1)
                    b = full(sx)
                    act.activation(xs[:, c % 2, :], psum[:, b, :], ACT.Copy).then_inc(bank_free[b], 1)
                    act.wait_ge(scy_made, i * 4 + (c + 1))
                    round_(row(scy[0], i * 4 + c, 0, S), sct[:, c % 2, :])
            splits[0] += KT
            with repeat(act, 2, [(gm, 4)]) as i:
                for c in range(4):
                    b = full(gm.take())
                    act.activation(row(merged, i * 4 + c, 0, S), psum[:, b, :], ACT.Sigmoid).then_inc(bank_free[b], 1)
            at.take()
            for _ in range(KT):
                gm.take()
            act.wait_ge(cf_centred, KT)
            norm(cfc, dst=None)
            for k in range(KT):
                act.wait_ge(norm_out, KT * (norms[0] - 1) + k + 1)
                act.activation(cfc[:, k, :], cfc[:, k, :], ACT.Silu, bias=vec("ln_b", k)).then_inc(cf_silu, 1)
            for k in range(KT):
                act.wait_ge(cf_silu, k + 1)
                round_(cfs[0][:, k, :], cfc[:, k, :])
            splits[0] += KT
            with repeat(act, 4, [(gm, 4)]):
                for c in range(2):
                    gcf, ycf = gm.take(), gm.take()
                    b = full(gcf)
                    act.wait_ge(bank_free[ycf[0]], ycf[1] + 1)
                    act.activation(xs[:, c, :], psum[:, b, :], ACT.Sigmoid).then_inc(bank_free[b], 1)
            for k in range(KT):
                act.wait_ge(merged_done, k + 2)
                if k == 0:
                    act.wait_ge(merged_done, KT + 1)
                round_(op[0][:, k, 0:S], merged[:, k, :])
            splits[0] += KT
            act.dma_start(memT, memT_d).then_inc(mem_loaded, 16)
            made = [[gm.take()] for _ in range(KT)]
            act.wait_ge(mem_loaded, 32)
            norm(memT, ((0, MEM),), dst=memN)
            norm(xT, off=META, made=made)

            with repeat(act, 2, [(gm, 12), (at, 20)]) as i:
                for h in range(2):
                    ks, vs, qs = ([gm.take() for _ in range(2)] for _ in range(3))
                    for d in range(XA_DT):
                        b = full(ks[d])
                        act.activation(xk[:, h, d * MEM:(d + 1) * MEM], psum[:, b, 0:MEM], ACT.Copy)\
                            .then_inc(bank_free[b], 1)
                    for d in range(XA_DT):
                        b = full(qs[d])
                        act.activation(xq[:, h, d * S:(d + 1) * S], psum[:, b, :], ACT.Copy)\
                            .then_inc(bank_free[b], 1)
                    for j in range(QT):
                        b = at.take()[0]
                        act.wait_ge(xa_bias, i * (2 * QT) + (h * QT + j + 1))
                        act.activation(xp[:, h, j * MEM:(j + 1) * MEM], psum[:, b, 0:MEM], ACT.Exp,
                                       bias=xneg[:, h, j:j + 1], scale=XA_SCALE, accum_out=xsum[:, h, j:j + 1])\
                            .then_inc(bank_free[b], 1)
                    for j in range(QT):
                        b = full(at.take())
                        act.activation(xpt[:, h, :].rearrange("p (t q) -> p t q", t=MT)[:, :, j * P:(j + 1) * P],
                                       psum[:, b, 0:MEM].rearrange("p (t q) -> p t q", t=MT), ACT.Copy)\
                            .then_inc(bank_free[b], 1)
                    for e in range(XA_DT):
                        b = full(at.take())
                        act.activation(row(oT, i * 4 + (2 * h + e), 0, S), psum[:, b, :], ACT.Copy)\
                            .then_inc(bank_free[b], 1)
            for k in range(KT):
                if k == 0:
                    drained(at)
                round_(op[0][:, k, 0:S], oT[:, k, :])
            splits[0] += KT
            act.dma_start(subk, subk_d).then_inc(subk_loaded, 16)
            norm(xT, off=META, made=[[gm.take()] for _ in range(KT)])
            with repeat(act, 4, [(gm, 4), (at, 4)]):
                for j in range(4):
                    b = full(gm.take())
                    act.activation(pq[:, j, :], psum[:, b, :], ACT.Copy).then_inc(bank_free[b], 1)
                    at.take()
            for tt in range(QT):
                for q in range(2):
                    b = full(at.take())
                    act.activation(hrow[:, tt, q * 512:(q + 1) * 512], psum[:, b, :], ACT.Copy)\
                        .then_inc(bank_free[b], 1)

            def gate_exps(tt):
                act.wait_ge(gate_in, tt + 1)
                act.activation(fin_e, fin_bf, ACT.Exp).then_inc(gate_exp, 1)

            gate_exps(0)
            turns = PICKS // TURN
            for tt in range(QT):
                banks = [at.take(), at.take()]
                for quarter in range(4):
                    if quarter == 2 and tt + 1 < QT:
                        gate_exps(tt + 1)
                    first = tt * turns + quarter * turns // 4
                    with act.Fori(first, first + turns // 4) as i:
                        for g in range(4):
                            slots = [g % 2 * GROUP + j for j in range(GROUP)]
                            act.wait_ge(u_used[slots[-1]], i * 2 + (g // 2 + 2))
                            act.activation(acts[:, g, :], dots[:, g, :], ACT.Gelu).then_inc(gelu_done, 1)
                            act.wait_ge(coef_done, i * 4 + (g + 1))
                            for j, slot in enumerate(slots):
                                act.wait_ge(v_used[slot], i * 2 + (g // 2 + 1))
                                act.activation(diag[:, slot, :], ident[:, :], ACT.Copy, scale=coefs[:, g, j:j + 1])\
                                    .then_inc(diag_done[slot], 1)
                for q in range(2):
                    b = full(banks[q])
                    if tt:
                        pb, pn = before[q]
                        act.wait_ge(bank_full[pb], pn + 1)
                    act.activation(out_rows[:, q * 512:(q + 1) * 512], psum[:, b, :], ACT.Copy)\
                        .then_inc(bank_free[b], 1)
                before = [at.take(), at.take()]
            drained(at)
            norm(xT, off=META, dst=None)

            def swiglu(parts, off, **how):
                T = parts[-1][0] + parts[-1][1]
                norm(xT, parts, off, **how)
                with repeat(act, FT // 2, [(gm, 4 * len(parts))]) as i:
                    for c in range(2):
                        ups = [gm.take() for _ in parts]
                        for a, n in parts:
                            b = full(gm.take())
                            act.activation(silu[:, c, a:a + n], psum[:, b, 0:n], ACT.Silu)\
                                .then_inc(bank_free[b], 1)
                        for b, n in ups:
                            act.wait_ge(bank_free[b], n + 2)
                        round_(row(hid[0], i * 2 + c, 0, T), hid_new[:, c, 0:T])
                splits[0] += FT
                return [[gm.take() for _ in parts] for _ in range(KT)]

            made = swiglu(BLOCK2, 0, after_norm=True)
            norm(xT, BLOCK2, made=made, squares=sq_hid)
            for v, a in ((cos_i, 4), (sin_i, 5)):
                act.dma_start(v, consts_d[:, TABLES + a * T2:TABLES + (a + 1) * T2]).then_inc(mixer_loaded, 16)
            act.dma_start(wi, wi_d).then_inc(mixer_loaded, 16)
            for _ in range(5):
                gm.take()
            at.take()
            for j in range(1, QT):
                for h in range(IDX_HEADS):
                    n = (j - 1) * IDX_HEADS + h
                    b = full(at.take())
                    if n >= 2:
                        act.wait_ge(relu_read, n - 1)
                    act.activation(relu[:, h % 2, 0:(j + 1) * P], psum[:, b, 0:(j + 1) * P], ACT.Relu)\
                        .then_inc(bank_free[b], 1)
            act.wait_ge(index_scored, 1)
            for v, a in ((cos_r, 0), (sin_r, 1)):
                act.dma_start(v, consts_d[:, TABLES + a * T2:TABLES + (a + 1) * T2]).then_inc(mixer_loaded, 16)
            act.dma_start(decay, consts_d[:, DECAY:DECAY + S]).then_inc(decay_loaded, 16)
            act.dma_start(decay_m, consts16_d[:, 0:S]).then_inc(decay_loaded, 16)
            with repeat(act, RET_HEADS, [(gm, 12), (at, 12)]) as i:
                for _ in range(4):
                    gm.take()
                at.take()
                vm = at.take()
                for t in range(QT):
                    b = full(gm.take())
                    act.activation(rv[:, t, :], psum[:, b, :], ACT.Copy).then_inc(bank_free[b], 1)
                b = full(vm)
                act.activation(rvm, psum[0:META, b, :], ACT.Copy).then_inc(bank_free[b], 1)
                for e in range(4):
                    b = full(gm.take())
                    act.activation(rg[:, e, :], psum[:, b, :], ACT.Silu).then_inc(bank_free[b], 1)
                for _ in range(5):
                    at.take()
                ys = []
                for e in range(4):
                    ys.append(at.take())
                    b = full(ys[-1])
                    act.activation(ry[:, e, :], psum[:, b, :], ACT.Copy).then_inc(bank_free[b], 1)
                act.dma_start(decay, consts_d[:, bass.ds(i * S + (DECAY + S), S)]).then_inc(decay_loaded, 16)
                act.dma_start(decay_m, consts16_d[:, bass.ds(i * S + S, S)]).then_inc(decay_loaded, 16)
                for e in range(4):
                    b, n = ys[e]
                    act.wait_ge(bank_free[b], n + 2)
                    act.activation(rsq[:, e, 0:S], ry[:, e, :], ACT.Square).then_inc(ret_sq, 1)
                at.take()
                act.wait_ge(ret_ms, i + 1)
                act.activation(norm_rs[:, 0:S], norm_ms[:, 0:S], ACT.Sqrt).then_inc(ret_root, 1)
            act.wait_ge(ret_done, 4 * RET_HEADS)
            act.wait_ge(decay_loaded, 32 * (RET_HEADS + 1))
            for v, a in ((cos_a, 2), (sin_a, 3)):
                act.dma_start(v, consts_d[:, TABLES + a * T2:TABLES + (a + 1) * T2]).then_inc(mixer_loaded, 16)
            for k in range(4 * RET_HEADS):
                round_(yr_s[0][:, k, :], yr[:, k, :])
                if k % 2:
                    b = full(gm.take())
                    act.activation(gs[:, k // 2, :], psum[:, b, :], ACT.Sigmoid).then_inc(bank_free[b], 1)
            splits[0] += 4 * RET_HEADS
            for _ in range(8):
                gm.take()
            for group in range(2):
                vm = at.take()
                for t in range(QT):
                    b = full(gm.take())
                    act.activation(av[:, t, group * S:(group + 1) * S], psum[:, b, :], ACT.Copy)\
                        .then_inc(bank_free[b], 1)
                b = full(vm)
                act.activation(avm[:, group * S:(group + 1) * S], psum[0:META, b, :], ACT.Copy)\
                    .then_inc(bank_free[b], 1)
            drained(at)
            drained(gm)
            with repeat(act, ATT_HEADS // 4, [(gm, 12), (at, 48)]) as i:
                for h in range(4):
                    act.activation(av_h, av[:, :, bass.ds(i * (4 * P) + h * P, P)], ACT.Copy).then_inc(val_step, 1)
                    act.wait_ge(val_step, i * 4 + (h + 1))
                    act.activation(avm_h, avm[:, bass.ds(i * (4 * P) + h * P, P)], ACT.Copy).then_inc(values_here, 1)
                    gm.take()
                    at.take()
                    gm.take()
                    b = full(gm.take())
                    act.activation(row(sga, i * 4 + h, 0, S), psum[:, b, :], ACT.Sigmoid).then_inc(bank_free[b], 1)
                    at.take()
                    for j in range(QT):
                        at.take()
                        act.wait_ge(att_bias, i * (4 * QT) + (h * QT + j + 1))
                        act.activation(ap_[:, j, 0:META + (j + 1) * P], ap_[:, j, 0:META + (j + 1) * P], ACT.Exp,
                                       bias=aneg[:, j:j + 1], accum_out=asum[:, j:j + 1]).then_inc(att_exp, 1)
                    for j in range(QT):
                        b = full(at.take())
                        act.activation(apt[:, 0:j + 1, j * P:(j + 1) * P],
                                       psum[:, b, 0:(j + 1) * P].rearrange("p (t n) -> p t n", t=j + 1), ACT.Copy)\
                            .then_inc(bank_free[b], 1)
                    b = full(at.take())
                    act.activation(aptm, psum[0:META, b, :], ACT.Copy).then_inc(bank_free[b], 1)
                    b = full(at.take())
                    act.activation(row(oT2, i * 4 + h, 0, S), psum[:, b, :], ACT.Copy).then_inc(bank_free[b], 1)
            drained(at)
            for k in range(KT):
                round_(op[0][:, k, 0:S], oT2[:, k, :])
            splits[0] += KT
            for _ in range(8):
                gm.take()
            act.wait_ge(merged_done, 2 * KT + 1)
            for k in range(KT):
                round_(op[0][:, k, 0:S], merged[:, k, :])
            splits[0] += KT
            made = [[gm.take()] for _ in range(KT)]
            made = swiglu(FULL, META, made=made)
            norm(xT, off=META, dst=None, made=made, squares=sq_hid)
            totals.append((gm.value(), at.value()))

        @block.vector
        def _(dve):
            gm, at = Ring(4), Ring(4, 4)
            chain = Chain(dve, dve_step)
            step, sync = chain.step, chain.wait
            norms = [0]
            splits = Counter()

            def sync_apart():
                sync()
                dve.sem_inc(dve_passed, 1)

            def full(bn):
                dve.wait_ge(bank_full[bn[0]], bn[1] + 1)
                return bn[0]

            def remainder(dst, src, high):
                splits.k += 1
                dve.wait_ge(rounded, splits.value())
                dve.tensor_tensor(dst, src, high.bitcast(F32), ALU.subtract).then_inc(split, 1)

            def sum_square(k, T, squares=sq):
                if k:
                    dve.wait_ge(norm_sq, KT * norms[0] + k + 1)
                    if k > 1:
                        sync()
                    ins = dve.tensor_tensor(norm_rs[:, 0:T], squares[:, 0, 0:T] if k == 1 else norm_rs[:, 0:T],
                                            squares[:, k, 0:T], ALU.add)
                    if k < KT - 1:
                        step(ins)
                    else:
                        ins.then_inc(tiles_summed, 1)

            squared = [0]

            def norm(src, dst, gain, parts=FULL, off=0, dst_off=0, pair=None, squares=sq):
                T = parts[-1][0] + parts[-1][1]
                for k in range(squared[0], KT):
                    sum_square(k, T, squares)
                squared[0] = 0
                for a, n in parts:
                    b = full(at.take())
                    m = dve.tensor_scalar(norm_ms[:, a:a + n], psum[:, b, 0:n], 1.0 / D, EPS, ALU.mult, ALU.add)
                    m.then_inc(bank_free[b], 1)
                drained(at)
                dve.sem_inc(norm_mean, 1)
                dve.wait_ge(norm_root, norms[0] + 1)
                step(dve.reciprocal(norm_ms[:, 0:T], norm_rs[:, 0:T]))
                sync()
                def rest(k):
                    if pair:
                        remainder(pair[1][:, k, 0:T], dst[:, k, 0:T], pair[0][:, k, 0:T])

                for k in range(KT):
                    dve.scalar_tensor_tensor(out=dst[:, k, dst_off:dst_off + T], in0=src[:, k, off:off + T],
                                             scalar=vec(gain, k), in1=norm_ms[:, 0:T], op0=ALU.mult, op1=ALU.mult)\
                        .then_inc(norm_out, 1)
                    if k:
                        rest(k - 1)
                rest(KT - 1)
                norms[0] += 1

            def add_to_stream(scale=1.0, parts=FULL, off=META, summing=True, squares=sq):
                T = parts[-1][0] + parts[-1][1]
                for k in range(KT):
                    for a, n in parts:
                        b = full(gm.take())
                        x = xT[:, k, off + a:off + a + n]
                        dve.scalar_tensor_tensor(out=x, in0=psum[:, b, 0:n], scalar=scale, in1=x, op0=ALU.mult,
                                                 op1=ALU.add).then_inc(bank_free[b], 1)
                    if summing and k > 1:
                        sum_square(k - 1, T, squares)
                if summing:
                    squared[0] = KT - 1

            def drained(ring):
                for b, n in ring.taken():
                    if n:
                        dve.wait_ge(bank_free[b], n + 1)

            dve.sem_inc(merged_done, 1)
            step(dve.memset(cfp[:, :, 0:CF_K - 1], 0.0))
            step(dve.memset(scp[:, :, 0:SC_K - 1], 0.0))
            step(dve.memset(zeros[:, :], 0.0))
            dve.memset(zero[:, :], 0.0).then_inc(cleared, 1)
            sync()
            dve.wait_ge(loaded, 16 * 6)
            norm(xT, sq, "norm_mix", off=META, pair=op)

            with repeat(dve, 2, [(gm, 20), (chain, 4 * 35), (splits, 4)]) as i:
                for c in range(4):
                    a, g, sc, sx, sb_ = (gm.take() for _ in range(5))
                    h = c % 2
                    b = full(a)
                    dve.wait_ge(bank_free[g[0]], g[1] + 2)
                    dve.scalar_tensor_tensor(out=cfp[:, h, CF_K - 1:], in0=psum[:, b, :], scalar=vec_at("b1a", i, 4, c),
                                             in1=sg[:, h, :], op0=ALU.add, op1=ALU.mult).then_inc(bank_free[b], 1)
                    b = full(sc)
                    dve.wait_ge(bank_free[sx[0]], sx[1] + 2)
                    dve.tensor_tensor(scp[:, h, SC_K - 1:], psum[:, b, :], xs[:, h, :], ALU.mult)\
                        .then_inc(bank_free[b], 1)
                    dve.wait_ge(bank_free[b], sc[1] + 2)
                    for t in range(SC_K):
                        w = vec_at("sc_w", i, 4 * SC_K, c * SC_K + t)
                        if t == 0:
                            step(dve.tensor_scalar(sct[:, h, :], scp[:, h, 0:S], w, None, ALU.mult))
                        else:
                            step(dve.scalar_tensor_tensor(out=sct[:, h, :], in0=scp[:, h, t:t + S], scalar=w,
                                                          in1=sct[:, h, :], op0=ALU.mult, op1=ALU.add))
                        sync()
                    b = full(sb_)
                    dve.tensor_tensor(sct[:, h, :], psum[:, b, :], sct[:, h, :], ALU.mult).then_inc(bank_free[b], 1)
                    dve.wait_ge(bank_free[b], sb_[1] + 2)
                    dve.sem_inc(scy_made, 1)
                    dve.wait_ge(bank_free[a[0]], a[1] + 2)
                    for t in range(CF_K):
                        acc = acc_o if t % 2 else acc_e
                        w = vec_at("cf_w", i, 4 * CF_K, c * CF_K + t)
                        if t > 1:
                            sync(1)
                        if t < 2:
                            step(dve.tensor_scalar(acc, cfp[:, h, t:t + S], w, None, ALU.mult))
                        else:
                            step(dve.scalar_tensor_tensor(out=acc, in0=cfp[:, h, t:t + S], scalar=w, in1=acc,
                                                          op0=ALU.mult, op1=ALU.add))
                    sync()
                    step(dve.scalar_tensor_tensor(out=row(cfc, i * 4 + c, 0, S), in0=acc_e,
                                                  scalar=vec_at("cf_b", i, 4, c), in1=acc_o, op0=ALU.add, op1=ALU.add))
                    sync()
                    remainder(row(scy[1], i * 4 + c, 0, S), sct[:, h, :], row(scy[0], i * 4 + c, 0, S))
            for _ in range(KT):
                gm.take()
            for k in range(1, KT):
                sync()
                step(dve.tensor_tensor(norm_rs[:, 0:S], cfc[:, 0, :] if k == 1 else norm_rs[:, 0:S], cfc[:, k, :],
                                       ALU.add))
            sync()
            dve.sem_inc(tiles_summed, 1)
            bn = at.take()
            b = full(bn)
            dve.tensor_scalar(mu, psum[:, b, :], 1.0 / D, None, ALU.mult).then_inc(bank_free[b], 1)
            dve.wait_ge(bank_free[b], bn[1] + 2)
            for k in range(KT):
                dve.tensor_tensor(cfc[:, k, :], cfc[:, k, :], mu, ALU.subtract).then_inc(cf_centred, 1)
            dve.wait_ge(cf_centred, KT)
            drained(gm)
            for k in range(KT):
                b = full(gm.take())
                dve.tensor_tensor(merged[:, k, :], psum[:, b, :], merged[:, k, :], ALU.mult).then_inc(bank_free[b], 1)
                sum_square(k, S)
            squared[0] = KT
            norm(cfc, cfc, "ln_g")
            for k in range(KT):
                remainder(cfs[1][:, k, :], cfc[:, k, :], cfs[0][:, k, :])
            drained(gm)
            with repeat(dve, 4, [(gm, 4)]) as i:
                for c in range(2):
                    gcf, ycf = gm.take(), gm.take()
                    b = full(ycf)
                    dve.wait_ge(bank_free[gcf[0]], gcf[1] + 2)
                    dve.wait_ge(merged_done, i * 2 + (c + 1))
                    dve.scalar_tensor_tensor(out=acc_o, in0=psum[:, b, :], scalar=vec_at("pw2_b", i, 2, c),
                                             in1=xs[:, c, :], op0=ALU.add, op1=ALU.mult).then_inc(bank_free[b], 1)
                    dve.wait_ge(bank_free[b], ycf[1] + 2)
                    m = row(merged, i * 2 + c, 0, S)
                    dve.tensor_tensor(m, m, acc_o, ALU.add).then_inc(merged_done, 1)
            for k in range(KT):
                remainder(op[1][:, k, 0:S], merged[:, k, :], op[0][:, k, 0:S])

            norm(memT, sq, "norm_mem", ((0, MEM),), pair=memN)
            add_to_stream()
            norm(xT, sq, "norm_xa", off=META, pair=op)
            with repeat(dve, 2, [(gm, 12), (at, 20), (chain, 4 * QT)]) as i:
                for h in range(2):
                    ks, vs, qs = ([gm.take() for _ in range(2)] for _ in range(3))
                    for t in range(MT):
                        b = full(vs[t])
                        dve.tensor_copy(xv[:, h, t * XA_DT * P:(t + 1) * XA_DT * P], psum[:, b, 0:XA_DT * P])\
                            .then_inc(bank_free[b], 1)
                    scores = [at.take() for _ in range(QT)]
                    for j in range(QT):
                        b = full(scores[j])
                        step(dve.reduce_max(xmax[:, h, j:j + 1], psum[:, b, 0:MEM], AX))
                        sync()
                        dve.tensor_scalar(xneg[:, h, j:j + 1], xmax[:, h, j:j + 1], -XA_SCALE, None, ALU.mult)\
                            .then_inc(xa_bias, 1)
                    for j in range(QT):
                        b, n = scores[j]
                        dve.wait_ge(bank_free[b], n + 2)
                        step(dve.reciprocal(xinv[:, h, j:j + 1], xsum[:, h, j:j + 1]))
                        sync()
                        dve.tensor_scalar(xp[:, h, j * MEM:(j + 1) * MEM], xp[:, h, j * MEM:(j + 1) * MEM],
                                          xinv[:, h, j:j + 1], None, ALU.mult).then_inc(xa_probs, 1)
                    for _ in range(QT + XA_DT):
                        at.take()
            for k in range(KT):
                remainder(op[1][:, k, 0:S], oT[:, k, :], op[0][:, k, 0:S])
            add_to_stream()
            drained(gm)
            norm(xT, sq, "norm_peer", off=META, pair=op)

            with repeat(dve, 4, [(gm, 4), (at, 4)]) as i:
                for j in range(4):
                    gm.take()
                    b = full(at.take())
                    dve.tensor_copy(sub_s[:, :, bass.ds(i * 4 + j, 1), :].rearrange("p t a n -> p t (a n)"),
                                    psum[:, b, :].rearrange("p (t n) -> p t n", t=QT)).then_inc(bank_free[b], 1)
            drained(at)
            for _ in range(2 * QT):
                at.take()
            ids = tk_f.rearrange("p (h s) k -> p h s k", s=2)
            halves = tk_v.rearrange("p (h s) k -> p h s k", s=2)
            four = [P, PEER_HEADS, TOPK, TOPK]

            def keep_first(tt):
                tk_in = sub_s[:, tt]
                for q in range(B2):
                    step(dve.max(tk_v[:, q, 0:8], tk_in[:, q, :]))
                sync()
                for q in range(B2):
                    step(dve.max_index(tk_i[:, q, 0:8], tk_v[:, q, 0:8], tk_in[:, q, :]))
                    step(dve.match_replace(tk_wk[:, q, :], tk_v[:, q, 0:8], tk_in[:, q, :], FLOOR))
                sync()

            def keep_second(tt):
                for q in range(B2):
                    step(dve.max(tk_v[:, q, 8:16], tk_wk[:, q, :]))
                sync()
                for q in range(B2):
                    step(dve.max_index(tk_i[:, q, 8:16], tk_v[:, q, 8:16], tk_wk[:, q, :]))
                cand = sub_s[:, tt].rearrange("p (h a) n -> p h (a n)", h=PEER_HEADS)
                step(dve.tensor_tensor(cand.rearrange("p h (a b) -> p h a b", a=TOPK),
                                       halves[:, :, 0, :].unsqueeze(3).to_broadcast(four),
                                       halves[:, :, 1, :].unsqueeze(2).to_broadcast(four), ALU.add))
                sync()
                step(dve.tensor_copy(tk_f, tk_i))

            def keep_sums(tt):
                cand = sub_s[:, tt].rearrange("p (h a) n -> p h (a n)", h=PEER_HEADS)
                for h in range(PEER_HEADS):
                    step(dve.max(fin_v[:, h, 0:8], cand[:, h, :]))
                sync()
                for h in range(PEER_HEADS):
                    step(dve.max_index(fin_p[:, h, 0:8], fin_v[:, h, 0:8], cand[:, h, :]))
                    step(dve.match_replace(cand_wk[:, h, :], fin_v[:, h, 0:8], cand[:, h, :], FLOOR))
                sync()
                for h in range(PEER_HEADS):
                    step(dve.max(fin_v[:, h, 8:16], cand_wk[:, h, :]))
                sync()
                for h in range(PEER_HEADS):
                    step(dve.max_index(fin_p[:, h, 8:16], fin_v[:, h, 8:16], cand_wk[:, h, :]))
                step(dve.tensor_tensor(fin_bf, fin_v, fin_v[:, :, 0:1].to_broadcast([P, PEER_HEADS, TOPK]),
                                       ALU.subtract))
                sync()
                dve.sem_inc(gate_in, 1)
                dve.wait_ge(gate_exp, tt + 1)
                step(dve.reduce_sum(fin_s, fin_e, AX))
                sync()
                step(dve.reciprocal(fin_r, fin_s))
                sync()
                step(dve.tensor_tensor(gates[:, tt, :].rearrange("p (h k) -> p h k", h=PEER_HEADS),
                                       fin_e, fin_r.unsqueeze(2).to_broadcast([P, PEER_HEADS, TOPK]), ALU.mult))

            def name_experts(tt):
                onehot = sub_s[:, tt].rearrange("p a (b n) -> p (a b) n", n=TOPK)
                hot = onehot.rearrange("p (h k) n -> p h k n", h=PEER_HEADS)
                step(dve.tensor_scalar(fin_a, fin_p, 4, None, ALU.logical_shift_right))
                step(dve.tensor_scalar(fin_b, fin_p, 15, None, ALU.bitwise_and))
                sync()
                step(dve.tensor_copy(fin_af, fin_a))
                step(dve.tensor_copy(fin_bf, fin_b))
                for s, (place, key) in enumerate(((fin_af, fin_i0), (fin_bf, fin_i1))):
                    sync()
                    step(dve.tensor_tensor(
                        onehot, iota16.unsqueeze(1).to_broadcast([P, PICKS, TOPK]),
                        place.rearrange("p a b -> p (a b)").unsqueeze(2).to_broadcast([P, PICKS, TOPK]), ALU.is_equal))
                    sync()
                    step(dve.tensor_tensor(hot, hot, ids[:, :, s, :].unsqueeze(2).to_broadcast(four), ALU.mult))
                    sync()
                    step(dve.reduce_sum(key.rearrange("p a b -> p (a b)"), onehot, AX))
                sync()
                step(dve.scalar_tensor_tensor(out=fin_af, in0=fin_i0, scalar=float(P), in1=fin_i1,
                                              op0=ALU.mult, op1=ALU.add))
                sync()
                step(dve.tensor_copy(eidx[:, tt, :], fin_af.rearrange("p a b -> p (a b)")))
                sync()
                dve.sem_inc(picked, 1)

            choice = (keep_first, keep_second, keep_sums, name_experts)
            for work_on in choice[:-1]:
                work_on(0)
            drained(at)
            name_experts(0)
            turns = PICKS // TURN
            for tt in range(QT):
                banks = [at.take(), at.take()]
                turned = [at.take(), at.take()]
                gate_groups = gates[:, tt, :].rearrange("p (g j) -> p g j", j=GROUP)
                for quarter in range(4):
                    if tt + 1 < QT:
                        choice[quarter](tt + 1)
                    first = tt * turns + quarter * turns // 4
                    with dve.Fori(first, first + turns // 4) as i:
                        for g in range(4):
                            for j in range(GROUP):
                                slot = g % 2 * GROUP + j
                                dve.wait_ge(u_landed[slot], i * 32 + (g // 2 * 16 + 16))
                                if slot:
                                    dve.wait_ge(u_used[slot - 1], i * 2 + (g // 2 + 2))
                                else:
                                    dve.wait_ge(u_used[SLOTS - 1], i * 2 + (g // 2 + 1))
                                dve.tensor_tensor_reduce(dump, u_rows[:, slot, :], hrow[:, tt, :], 1.0, 0.0, ALU.mult,
                                                         ALU.add, dots[:, g, j:j + 1]).then_inc(u_used[slot], 1)
                            dve.wait_ge(gelu_done, i * 4 + (g + 1))
                            dve.tensor_tensor(coefs[:, g, :], acts[:, g, :],
                                              gate_groups[:, bass.ds(i * 4 + (g - tt * turns * 4), 1), :]
                                              .rearrange("p a j -> p (a j)"), ALU.mult).then_inc(coef_done, 1)
                for q in range(2):
                    b = full(turned[q])
                    x = xT[:, 4 * q:4 * q + 4, META + tt * P:META + (tt + 1) * P]
                    dve.tensor_tensor(x, psum[:, b, :].rearrange("p (k n) -> p k n", k=4), x, ALU.add)\
                        .then_inc(bank_free[b], 1)
            norm(xT, xT, "final1", off=META, dst_off=META)

            def swiglu(gain, parts, off):
                norm(xT, sq, gain, parts, off, pair=op)
                T = parts[-1][0] + parts[-1][1]
                with repeat(dve, FT // 2, [(gm, 4 * len(parts)), (splits, 2)]) as i:
                    for c in range(2):
                        ups, gts = ([gm.take() for _ in parts] for _ in range(2))
                        for (a, n), u, g in zip(parts, ups, gts):
                            b = full(u)
                            dve.wait_ge(bank_free[g[0]], g[1] + 2)
                            dve.tensor_tensor(hid_new[:, c, a:a + n], psum[:, b, 0:n], silu[:, c, a:a + n],
                                              ALU.mult).then_inc(bank_free[b], 1)
                        remainder(row(hid[1], i * 2 + c, 0, T), hid_new[:, c, 0:T], row(hid[0], i * 2 + c, 0, T))
                add_to_stream(0.5, parts, off, squares=sq_hid)
                drained(gm)

            swiglu("ffn1", BLOCK2, 0)
            norm(xT, sq, "mix2", BLOCK2, pair=op, squares=sq_hid)
            dve.wait_ge(mixer_loaded, 16 * 3)

            def rope_blocks(dst, b, width, cos, sin, size, off, done_bank):
                t = rope_t[:, 0, 0:width]
                step(dve.tensor_tensor(dst, psum[:, b, 0:width], cos[:, off:off + width], ALU.mult))
                for r in range(0, P, size):
                    o = r + size if (r // size) % 2 == 0 else r - size
                    ins = dve.tensor_tensor(rope_t[o:o + size, 0, 0:width], psum[r:r + size, b, 0:width],
                                            sin[r:r + size, off:off + width], ALU.mult)
                    step(ins)
                sync()
                dve.sem_inc(bank_free[b], 1)
                step(dve.tensor_tensor(dst, dst, t, ALU.add))
                sync()

            for q in range(5):
                b = full(gm.take())
                rope_blocks(iq[:, q, :] if q < 4 else ik, b, S, cos_i, sin_i, 32, META, None)
                dve.sem_inc(idx_rope, 1)
            bn = at.take()
            b = full(bn)
            dve.tensor_copy(iw.rearrange("p t h -> p (t h)"), psum[:, b, 0:QT * IDX_HEADS]).then_inc(bank_free[b], 1)
            dve.wait_ge(bank_free[b], bn[1] + 2)
            for j in range(1, QT):
                w = (j + 1) * P
                for h in range(IDX_HEADS):
                    b, n = at.take()
                    dve.wait_ge(bank_free[b], n + 2)
                    if h == 0:
                        dve.tensor_scalar(score[:, j - 1, 0:w], relu[:, h % 2, 0:w], iw[:, j, h:h + 1], None,
                                          ALU.mult).then_inc(relu_read, 1)
                    else:
                        dve.wait_ge(relu_read, (j - 1) * IDX_HEADS + h)
                        dve.scalar_tensor_tensor(out=score[:, j - 1, 0:w], in0=relu[:, h % 2, 0:w],
                                                 scalar=iw[:, j, h:h + 1], in1=score[:, j - 1, 0:w],
                                                 op0=ALU.mult, op1=ALU.add).then_inc(relu_read, 1)
            dve.wait_ge(relu_read, 3 * IDX_HEADS)
            for j in range(1, QT):
                step(dve.tensor_scalar(work[:, j - 1, 0:(j + 1) * P], score[:, j - 1, 0:(j + 1) * P], IDX_SCALE, None,
                                       ALU.mult))
            sync()
            step(dve.tensor_scalar(relu[:, 0, 0:P], tri[:, :], -FAR, FAR, ALU.mult, ALU.add))
            sync()
            for j in range(1, QT):
                dg = work[:, j - 1, j * P:(j + 1) * P]
                step(dve.tensor_tensor(dg, dg, tri[:, :], ALU.mult))
            sync()
            for j in range(1, QT):
                dg = work[:, j - 1, j * P:(j + 1) * P]
                step(dve.tensor_tensor(dg, dg, relu[:, 0, 0:P], ALU.add))
            sync()
            dve.sem_inc(index_scored, 1)

            def keep_keys():
                for j in range(1, QT):
                    step(dve.max(top8[:, j - 1, :], work[:, j - 1, 0:(j + 1) * P]))
                sync_apart()
                for j in range(1, QT):
                    wk = work[:, j - 1, 0:(j + 1) * P]
                    step(dve.match_replace(wk, top8[:, j - 1, :], wk, TAKEN))
                sync_apart()

            dve.wait_ge(mixer_loaded, 16 * 5)

            def rope_pair(dst, a, b, width, off, tmp):
                c, s = cos_r[:, off:off + width], sin_r[:, off:off + width]
                (pa, fa), (pb, fb) = a, b
                step(dve.tensor_tensor(tmp[:, 0, 0:width], pa, c, ALU.mult))
                step(dve.tensor_tensor(tmp[:, 3, 0:width], pa, s, ALU.mult))
                step(dve.tensor_tensor(tmp[:, 1, 0:width], pb, s, ALU.mult))
                step(dve.tensor_tensor(tmp[:, 2, 0:width], pb, c, ALU.mult))
                sync()
                for f in dict.fromkeys((fa, fb)):
                    dve.sem_inc(bank_free[f], 1)
                step(dve.tensor_tensor(dst[:, 0, :], tmp[:, 0, 0:width], tmp[:, 1, 0:width], ALU.subtract))
                step(dve.tensor_tensor(dst[:, 1, :], tmp[:, 2, 0:width], tmp[:, 3, 0:width], ALU.add))
                sync()
                dve.sem_inc(ret_rope, 1)

            with repeat(dve, RET_HEADS, [(gm, 12), (at, 12), (chain, 18 + 1 + 4 + 3 + 6 * (KEEP // 8 // RET_HEADS))]) as i:
                q = [gm.take() for _ in range(2)]
                k = [gm.take() for _ in range(2)]
                km, vm = at.take(), at.take()
                vg = [gm.take() for _ in range(8)]
                b0, b1 = full(q[0]), full(q[1])
                rope_pair(rq, (psum[:, b0, :], b0), (psum[:, b1, :], b1), S, META, rt)
                b0, b1 = full(k[0]), full(k[1])
                rope_pair(rk, (psum[:, b0, :], b0), (psum[:, b1, :], b1), S, META, rt)
                b = full(km)
                rope_pair(rkm, (psum[:, b, 0:META], b), (psum[:, b, META:2 * META], b), META, 0, rtm)
                for _ in range(KEEP // 8 // RET_HEADS):
                    keep_keys()
                b = full(at.take())
                dve.wait_ge(decay_loaded, i * 32 + 32)
                dve.tensor_tensor(rpm, psum[0:META, b, :], decay_m, ALU.mult).then_inc(bank_free[b], 1)
                for s in range(QT):
                    b = full(at.take())
                    dve.tensor_tensor(rp[:, s, s * P:S], psum[:, b, 0:S - s * P], decay[:, 0:S - s * P],
                                      ALU.mult).then_inc(bank_free[b], 1)
                ys = [at.take() for _ in range(4)]
                for e in range(1, 4):
                    dve.wait_ge(ret_sq, i * 4 + (e + 1))
                    sync()
                    step(dve.tensor_tensor(rsq[:, 0, :], rsq[:, 0, :], rsq[:, e, :], ALU.add))
                sync()
                dve.sem_inc(ret_summed, 1)
                bn = at.take()
                b = full(bn)
                dve.tensor_scalar(norm_ms[:, 0:S], psum[:, b, :], 1.0 / RET_DV, EPS, ALU.mult, ALU.add)\
                    .then_inc(bank_free[b], 1)
                dve.wait_ge(bank_free[b], bn[1] + 2)
                dve.sem_inc(ret_ms, 1)
                dve.wait_ge(ret_root, i + 1)
                step(dve.reciprocal(norm_ms[:, 0:S], norm_rs[:, 0:S]))
                sync()
                for e in range(4):
                    step(dve.tensor_tensor(ry[:, e, :], ry[:, e, :], norm_ms[:, 0:S], ALU.mult))
                sync()
                for e in range(4):
                    b, n = vg[4 + e]
                    dve.wait_ge(bank_free[b], n + 2)
                    dve.tensor_tensor(row(yr, i * 4 + e, 0, S), ry[:, e, :], rg[:, e, :], ALU.mult)\
                        .then_inc(ret_done, 1)
            for j in range(1, QT):
                w = work[:, j - 1, 0:(j + 1) * P]
                step(dve.tensor_scalar(w, w, TAKEN, HIDE, ALU.not_equal, ALU.mult))
            step(dve.tensor_scalar(key_bias[:, 0, 0:P], tri[:, :], -HIDE, HIDE, ALU.mult, ALU.add))
            sync()
            for _ in range(KT):
                gm.take()
            for k in range(4 * RET_HEADS):
                remainder(yr_s[1][:, k, :], yr[:, k, :], yr_s[0][:, k, :])
            drained(gm)
            with repeat(dve, 2, [(gm, 4)]) as i:
                for c in range(4):
                    b = full(gm.take())
                    dve.tensor_tensor(row(merged, i * 4 + c, 0, S), psum[:, b, :], row(gs, i * 4 + c, 0, S), ALU.mult)\
                        .then_inc(bank_free[b], 1)
            for _ in range(2):
                at.take()
            for _ in range(2 * QT):
                gm.take()
            dve.wait_ge(mixer_loaded, 16 * 7)

            def rope_halves(dst, src, b, t, width, off, frees):
                step(dve.tensor_tensor(dst, src, cos_a[:, off:off + width], ALU.mult))
                step(dve.tensor_tensor(t[64:128], src[0:64], sin_a[0:64, off:off + width], ALU.mult))
                step(dve.tensor_tensor(t[0:64], src[64:128], sin_a[64:128, off:off + width], ALU.mult))
                sync()
                if frees:
                    dve.sem_inc(bank_free[b], 1)
                step(dve.tensor_tensor(dst, dst, t, ALU.add))
                sync()
                dve.sem_inc(att_rope, 1)

            with repeat(dve, ATT_HEADS // 4, [(gm, 12), (at, 48), (chain, 4 * (12 + 3 * QT))]) as i:
                for h in range(4):
                    q, k, g = gm.take(), gm.take(), gm.take()
                    kv = at.take()
                    b = full(q)
                    rope_halves(aq, psum[:, b, :], b, at_t[:, 0, :], S, META, True)
                    b = full(k)
                    rope_halves(ak[:, META:T2], psum[:, b, :], b, at_t[:, 1, :], S, META, True)
                    b = full(kv)
                    rope_halves(ak[:, 0:META], psum[:, b, 0:META], b, at_tm, META, 0, True)
                    mb = full(at.take())
                    for j in range(QT):
                        step(dve.tensor_scalar(ap_[:, j, 0:META], psum[:, mb, j * META:(j + 1) * META], ATT_SCALE, None,
                                               ALU.mult))
                    sync()
                    dve.sem_inc(bank_free[mb], 1)
                    for j in range(QT):
                        w = (j + 1) * P
                        bn = at.take()
                        b = full(bn)
                        dve.scalar_tensor_tensor(out=ap_[:, j, META:META + w], in0=psum[:, b, 0:w], scalar=ATT_SCALE,
                                                 in1=key_bias[:, j, 0:w], op0=ALU.mult, op1=ALU.add)\
                            .then_inc(bank_free[b], 1)
                        dve.wait_ge(bank_free[b], bn[1] + 2)
                        step(dve.reduce_max(amax[:, j:j + 1], ap_[:, j, 0:META + w], AX))
                        sync()
                        dve.tensor_scalar(aneg[:, j:j + 1], amax[:, j:j + 1], -1.0, None, ALU.mult).then_inc(att_bias, 1)
                    for j in range(QT):
                        w = META + (j + 1) * P
                        dve.wait_ge(att_exp, i * (4 * QT) + (h * QT + j + 1))
                        step(dve.reciprocal(ainv[:, j:j + 1], asum[:, j:j + 1]))
                        sync()
                        dve.tensor_scalar(ap_[:, j, 0:w], ap_[:, j, 0:w], ainv[:, j:j + 1], None, ALU.mult)\
                            .then_inc(att_probs, 1)
                    for _ in range(QT + 2):
                        at.take()
            for k in range(KT):
                remainder(op[1][:, k, 0:S], oT2[:, k, :], op[0][:, k, 0:S])
            drained(gm)
            with repeat(dve, 2, [(gm, 4)]) as i:
                for c in range(4):
                    bn = gm.take()
                    b = full(bn)
                    dve.tensor_tensor(at_y[:, c % 2, :], psum[:, b, :], row(sga, i * 4 + c, 0, S), ALU.mult)\
                        .then_inc(bank_free[b], 1)
                    dve.wait_ge(bank_free[b], bn[1] + 2)
                    m = row(merged, i * 4 + c, 0, S)
                    dve.tensor_tensor(m, m, at_y[:, c % 2, :], ALU.add).then_inc(merged_done, 1)
            for k in range(KT):
                remainder(op[1][:, k, 0:S], merged[:, k, :], op[0][:, k, 0:S])
            add_to_stream()
            drained(gm)
            swiglu("ffn2", FULL, META)
            norm(xT, sq, "final2", off=META, squares=sq_hid)
            totals.append((gm.value(), at.value()))

        @block.gpsimd
        def _(pool):
            def split_slab(turn, j, used=True):
                r = j % RAW
                pool.wait_ge(slab_landed[r], turn * (16 * READY // RAW) + (j // RAW * 16 + 16))
                if used:
                    pool.wait_ge(slab_used, turn * READY + (j - READY + 2))
                pool.tensor_tensor(slab_h[:, j, :], raw[:, r, :], zero[:, 0:1].to_broadcast([P, D]), ALU.add)\
                    .then_inc(slab_rounded, 1)
                pool.wait_ge(slab_rounded, turn * READY + (j + 1))
                pool.tensor_tensor(slab_l[:, j, :], raw[:, r, :], slab_h[:, j, :].bitcast(F32), ALU.subtract)\
                    .then_inc(slab_ready[j], 1)

            def split_slabs(a, b):
                while a < b and a % READY:
                    split_slab(a // READY, a % READY)
                    a += 1
                if b // READY > a // READY:
                    with pool.Fori(a // READY, b // READY) as turn:
                        for j in range(READY):
                            split_slab(turn, j)
                    a = b // READY * READY
                for n in range(a, b):
                    split_slab(n // READY, n % READY)

            pool.wait_ge(cleared, 1)
            for j in range(READY):
                split_slab(0, j, used=False)
            before = slabs_before_gathers[0] + READY - 2
            split_slabs(READY, before)
            for j in range(SLOTS):
                pool.sem_inc(u_used[j], 1)
                pool.sem_inc(v_used[j], 1)
            turns = PICKS // TURN
            for tt in range(QT):
                pool.wait_ge(picked, tt + 1)
                picks = eidx[:, tt, :].rearrange("p (g j) -> p g j", j=GROUP)
                with pool.Fori(tt * turns, (tt + 1) * turns) as i:
                    for g in range(4):
                        pool.tensor_copy(pick[:, g, :], picks[:, bass.ds(i * 4 + (g - tt * turns * 4), 1), :]
                                         .rearrange("p a j -> p (a j)")).then_inc(pick_copied, 1)
                        pool.wait_ge(pick_copied, i * 4 + (g + 1))
                        for j in range(GROUP):
                            slot = g % 2 * GROUP + j
                            index = bass.IndirectOffsetOnAxis(pick[:, g, j:j + 1], 0)
                            pool.wait_ge(u_used[slot], i * 2 + (g // 2 + 1))
                            pool.sem_inc(pool_passed, 1)
                            pool.indirect_dma_start(u_rows[:, slot, :], None, peer_u_d, index)\
                                .then_inc(u_landed[slot], 16)
                            pool.wait_ge(v_used[slot], i * 2 + (g // 2 + 1))
                            pool.sem_inc(pool_passed, 1)
                            pool.indirect_dma_start(v_rows[:, slot, :], None, peer_v_d, index)\
                                .then_inc(v_landed[slot], 16)

            split_slabs(before, n_slabs)

        assert totals[0][0] == n_slabs and totals[0][1:] == totals[1] == totals[2], totals


def lay_slabs(ins):
    out = []

    def wide(w, width, m):
        rows = D // width * P
        for r in range(0, D, rows):
            block = w[r:r + rows, m * width:(m + 1) * width].reshape(D // width, P, width)
            out.append(block.transpose(1, 0, 2).reshape(P, D))

    def cols(w, m, k0=0, nk=KT):
        block = np.zeros((P, KT, P), np.float32)
        block[:, 0:nk] = w[k0 * P:(k0 + nk) * P, m * P:(m + 1) * P].reshape(nk, P, P).transpose(1, 0, 2)
        out.append(block.reshape(P, D))

    w = ins["w_in"][0]
    sc_b, sc_c, sc_x, cf_a, cf_g, g_sc, g_cf = (w[:, n * D:(n + 1) * D] for n in range(7))
    for m in range(KT):
        for part in (cf_a, cf_g, sc_c, sc_x, sc_b):
            cols(part, m)
    for part in (g_sc, ins["sc_w_out"][0]):
        for m in range(KT):
            cols(part, m)
    for m in range(KT):
        for part in (g_cf, ins["cf_w_pw2"][0]):
            cols(part, m)
    for m in range(KT):
        cols(ins["w_mix_out"][0], m)
    kv, q = ins["w_kv"][0], ins["w_q"][0]
    for h in range(XA_HEADS):
        cols(kv[:, 0:D], 2 * h)
        cols(kv[:, 0:D], 2 * h + 1)
        wide(kv[:, D:2 * D], D // XA_HEADS, h)
        cols(q, 2 * h)
        cols(q, 2 * h + 1)
    for m in range(KT):
        cols(ins["w_xo"][0], m)
    for m in range(2 * PEER_HEADS):
        cols(ins["w_peer_q"][0], m)

    def swiglu(n):
        for f in range(FT):
            cols(ins[f"ffn{n}_w_up_2"][0], f)
            cols(ins[f"ffn{n}_w_gate_2"][0], f)
        for m in range(KT):
            for k0, nk in ((0, 8), (8, 8), (16, 6)):
                cols(ins[f"ffn{n}_w_down_2"][0], m, k0, nk)

    swiglu(1)
    w, parts, a = ins["w_in_2"][0], [], 0
    for n in (D, D, 2 * D, 2 * D, D, D, D, 512, 64, 8, D, D):
        parts.append(w[:, a:a + n])
        a += n
    rq, rk, rv, rg, aq, ak, av, iq, ik, iw, g_ret, g_att = parts
    for m in range(4):
        cols(iq, m)
    cols(np.concatenate([ik, ik], 1), 0)
    for h in range(RET_HEADS):
        for part in (rq, rk):
            cols(part, 2 * h)
            cols(part, 2 * h + 1)
        wide(rv, RET_DV, h)
        for m in range(4):
            cols(rg, 4 * h + m)
    for m in range(KT):
        cols(g_ret, m)
    for m in range(KT):
        cols(ins["w_ret_out_2"][0], m, 0)
        cols(ins["w_ret_out_2"][0], m, 8)
    wide(av, S, 0)
    wide(av, S, 1)
    for h in range(ATT_HEADS):
        for part in (aq, ak, g_att):
            cols(part, h)
    for name in ("w_att_out_2", "w_mix_out_2"):
        for m in range(KT):
            cols(ins[name][0], m)
    swiglu(2)
    return np.stack(out), np.ascontiguousarray(iw.reshape(KT, P, IDX_HEADS).transpose(1, 0, 2))


def tiles(x):
    return np.ascontiguousarray(x.T.reshape(-1, P, x.shape[0]).transpose(1, 0, 2))


def lay_vectors(ins):
    v = np.zeros((P, NVEC), np.float32)
    b1 = ins["cf_b_pw1"][0]
    for name, x in (("norm_mix", ins["norm_mix_g"]), ("b1a", b1[:D]), ("b1g", b1[D:]), ("cf_b", ins["cf_conv_b"]),
                    ("ln_g", ins["cf_ln_g"]), ("ln_b", ins["cf_ln_b"]), ("pw2_b", ins["cf_b_pw2"]),
                    ("norm_xa", ins["norm_xa_g"]), ("norm_mem", ins["norm_mem_g"]),
                    ("norm_peer", ins["norm_peer_g"]), ("final1", ins["final_norm_g"]),
                    ("ffn1", ins["ffn1_norm_2"]), ("mix2", ins["mix_norm_2"]), ("ffn2", ins["ffn2_norm_2"]),
                    ("final2", ins["final_norm_2"])):
        v[:, VECS[name]:VECS[name] + KT] = x.reshape(KT, P).T
    for name, x, taps in (("sc_w", ins["sc_conv_w"][0], SC_K), ("cf_w", ins["cf_conv_w"][0], CF_K)):
        v[:, VECS[name]:VECS[name] + KT * taps] = x.reshape(taps, KT, P).transpose(2, 1, 0).reshape(P, KT * taps)
    return v


def constants():
    c = np.zeros((P, NCONST), np.float32)
    c[:, 0:P] = np.eye(P)
    c[:, P:2 * P] = 1.0
    c[:, 2 * P:3 * P] = np.tril(np.ones((P, P)))
    c[:, 3 * P:FIXED] = np.arange(TOPK)
    pos = np.arange(T2, dtype=np.float32)
    at = TABLES
    for dim in (256, 128, 64):
        freq = (np.float32(THETA) ** (-np.arange(0, dim, 2, dtype=np.float32) / np.float32(dim))).astype(np.float32)
        angle = (freq[:, None] * pos[None, :]).astype(np.float32)
        half = dim // 2
        reps = P // half
        sign = np.ones(P) if dim == 256 else np.where((np.arange(P) // half) % 2 == 0, 1.0, -1.0)
        c[:, at:at + T2] = np.tile(np.cos(angle), (reps, 1))
        c[:, at + T2:at + 2 * T2] = np.tile(np.sin(angle), (reps, 1)) * sign[:, None]
        at += 2 * T2
    log_g = np.log1p(-(2.0 ** (-5.0 - np.arange(RET_HEADS))))
    key, query = np.arange(P)[:, None], np.arange(S)[None, :]
    meta = np.zeros((META, (RET_HEADS + 1) * S), np.float32)
    for h in range(RET_HEADS):
        d = query - key
        c[:, DECAY + h * S:DECAY + (h + 1) * S] = np.where(d >= 0, np.exp(log_g[h] * np.maximum(d, 0)), 0) * RET_DK ** -0.5
        meta[:, h * S:(h + 1) * S] = np.exp(log_g[h] * (query + META - key[:META])) * RET_DK ** -0.5
    return c, meta


def kernel(**inputs):
    import concourse.bacc as bacc
    from concourse.bass_utils import run_bass_kernel_spmd

    ins = {k: np.asarray(v) for k, v in inputs.items()}
    slabs, wi = lay_slabs(ins)
    consts, consts16 = constants()
    arrays = {
        "slabs": slabs,
        "xT": tiles(ins["x"][0]),
        "memT": tiles(ins["mem"][0]),
        "metaT": tiles(ins["meta_tokens_2"]),
        "vecs": lay_vectors(ins),
        "consts": consts,
        "consts16": consts16,
        "subkeys": np.ascontiguousarray(ins["peer_subkeys"][0].transpose(2, 0, 1)),
        "wi": wi,
        "peer_u": np.ascontiguousarray(ins["peer_u"][0]),
        "peer_v": np.ascontiguousarray(ins["peer_v"][0]),
    }
    nc = bacc.Bacc("TRN2", target_bir_lowering=False, num_devices=1)
    args = [nc.dram_tensor("in_" + name, a.shape, F32, kind="ExternalInput").ap() for name, a in arrays.items()]
    out = nc.dram_tensor("outT", (P, KT, S), F32, kind="ExternalOutput").ap()
    build(nc, *args, out, slabs.shape[0])
    got = run_bass_kernel_spmd(nc, [{"in_" + n: a for n, a in arrays.items()}], core_ids=[0]).results[0]["outT"]
    return np.ascontiguousarray(got.reshape(P, KT, S).transpose(2, 1, 0).reshape(1, S, D))
```
